# Optimizing a Trainium2 kernel written in Bass

```python
import jax, jax.numpy as jnp
from jax import lax
import numpy as np
import math
import jax
import jax.numpy as jnp

D_MODEL = 1024
BATCH = 1
SEQ = 256
DEPTH = 1

HEAD_DIM = 64
SCALE = HEAD_DIM ** -0.5
EPS = 1e-6
NEG = -1e30
DIL_PAIRS = ((128, 1), (512, 4), (2048, 16))
N_DIL_GROUPS = len(DIL_PAIRS)
HEADS_A = 8
WIDTH_A = N_DIL_GROUPS * HEADS_A * HEAD_DIM
OUT_A = HEADS_A * HEAD_DIM
ROT_DIM_A = HEAD_DIM // 4
THETA_PARTIAL = 500000.0
HEADS_B_Q = 8
HEADS_B_KV = 2
WIDTH_B_Q = HEADS_B_Q * HEAD_DIM
WIDTH_B_KV = HEADS_B_KV * HEAD_DIM
OUT_B = WIDTH_B_Q
Q_BLOCK = 128
GRID_W = 64
THETA_AXIAL = 10000.0
N_BRANCHES = 2
IN_COLS = 3 * WIDTH_A + WIDTH_B_Q + 2 * WIDTH_B_KV + N_BRANCHES * D_MODEL
N_EXPERTS = 32
TOP_K = 4
D_FF = 1024
SWIGLU_LIMIT = 7.0
SWIGLU_ALPHA = 1.702
EXPERT_BLOCK = 128


def rmsnorm(x, g):
    xf = x.astype(jnp.float32)
    y = xf * lax.rsqrt(jnp.mean(xf * xf, axis=-1, keepdims=True) + EPS)
    return (y * g).astype(x.dtype)

def rope(x, pos, theta):
    half = x.shape[-1] // 2
    inv = theta ** (-(jnp.arange(half, dtype=jnp.float32) / half))
    ang = pos.astype(jnp.float32)[:, None] * inv[None, :]
    cos, sin = jnp.cos(ang)[:, None, :], jnp.sin(ang)[:, None, :]
    xf = x.astype(jnp.float32)
    x1, x2 = xf[..., :half], xf[..., half:]
    return jnp.concatenate([x1 * cos - x2 * sin, x2 * cos + x1 * sin], axis=-1).astype(x.dtype)

def partial_rope(x, pos):
    return jnp.concatenate([rope(x[..., :ROT_DIM_A], pos, THETA_PARTIAL), x[..., ROT_DIM_A:]], axis=-1)

def axial_rope(x, row, col):
    h = x.shape[-1] // 2
    return jnp.concatenate([rope(x[..., :h], row, THETA_AXIAL), rope(x[..., h:], col, THETA_AXIAL)], axis=-1)

def _pad_axis3(x, lo, hi):
    return jnp.pad(x, ((0, 0), (0, 0), (0, 0), (lo, hi), (0, 0)))

def dilated_window_attention(q, k, v, window, dil):
    b, s, h, e = q.shape
    half = window // (2 * dil)
    L = s // dil
    nb = -(-L // half)
    lp = nb * half
    pad = lp - L

    def to_sub(t):
        return t.reshape(b, L, dil, h, e).transpose(0, 2, 3, 1, 4)

    qs, ks, vs = to_sub(q), to_sub(k), to_sub(v)
    qb = _pad_axis3(qs, 0, pad).reshape(b, dil, h, nb, half, e)

    def windows(t):
        tp = _pad_axis3(t, half, pad + half).reshape(b, dil, h, nb + 2, half, e)
        return jnp.concatenate([tp[:, :, :, :-2], tp[:, :, :, 1:-1], tp[:, :, :, 2:]], axis=4)

    kw, vw = windows(ks), windows(vs)
    sc = jnp.einsum('bdhnqe,bdhnke->bdhnqk', qb, kw).astype(jnp.float32) * SCALE
    blk = jnp.arange(nb)[:, None, None]
    qi = blk * half + jnp.arange(half)[None, :, None]
    ki = (blk - 1) * half + jnp.arange(3 * half)[None, None, :]
    valid = (jnp.abs(ki - qi) <= half) & (ki >= 0) & (ki < L)
    sc = jnp.where(valid, sc, NEG)
    lse = jax.nn.logsumexp(sc, axis=-1)
    p = jnp.exp(sc - lse[..., None])
    o = jnp.einsum('bdhnqk,bdhnke->bdhnqe', p.astype(v.dtype), vw)
    o = o.reshape(b, dil, h, lp, e)[:, :, :, :L].transpose(0, 3, 1, 2, 4).reshape(b, s, h, e)
    lse = lse.reshape(b, dil, h, lp)[..., :L].transpose(0, 3, 1, 2).reshape(b, s, h)
    return o, lse

def gqa_blocked_attention(q, k, v):
    b, s, hq, e = q.shape
    hkv = k.shape[2]
    g = hq // hkv
    nq = s // Q_BLOCK
    qb = q.reshape(b, nq, Q_BLOCK, hkv, g, e).transpose(1, 0, 3, 4, 2, 5)
    kt = k.transpose(0, 2, 1, 3)
    vt = v.transpose(0, 2, 1, 3)

    def one_block(qblk):
        sc = jnp.einsum('bkgqe,bkse->bkgqs', qblk, kt).astype(jnp.float32) * SCALE
        p = jax.nn.softmax(sc, axis=-1)
        return jnp.einsum('bkgqs,bkse->bkgqe', p.astype(vt.dtype), vt)

    ob = lax.map(one_block, qb)
    return ob.transpose(1, 0, 4, 2, 3, 5).reshape(b, s, hq * e)

def moe_ffn(h, w_router, b_router, w_gate_up, b_gate_up, w_down, b_down):
    t, d = h.shape
    logits = (h @ w_router).astype(jnp.float32) + b_router
    topv, idx = lax.top_k(logits, TOP_K)
    gates = jax.nn.softmax(topv, axis=-1)
    a = t * TOP_K
    flat_e = idx.reshape(a)
    flat_w = gates.reshape(a)
    flat_tok = jnp.arange(a) // TOP_K
    order = jnp.argsort(flat_e)
    e_s, tok_s, w_s = flat_e[order], flat_tok[order], flat_w[order]
    counts = jnp.bincount(flat_e, length=N_EXPERTS)
    starts = jnp.cumsum(counts) - counts
    padded = ((counts + EXPERT_BLOCK - 1) // EXPERT_BLOCK) * EXPERT_BLOCK
    pends = jnp.cumsum(padded)
    pstarts = pends - padded
    dest = pstarts[e_s] + (jnp.arange(a) - starts[e_s])
    p_rows = a + N_EXPERTS * EXPERT_BLOCK
    n_blk = p_rows // EXPERT_BLOCK
    block_e = jnp.clip(jnp.searchsorted(pends, jnp.arange(n_blk) * EXPERT_BLOCK, side='right'), 0, N_EXPERTS - 1)
    xbuf = jnp.zeros((p_rows, d), h.dtype).at[dest].set(h[tok_s])
    wbuf = jnp.zeros((p_rows,), jnp.float32).at[dest].set(w_s)
    tbuf = jnp.zeros((p_rows,), jnp.int32).at[dest].set(tok_s.astype(jnp.int32))

    def expert_block(args):
        xblk, e = args
        gu = xblk @ w_gate_up[e] + b_gate_up[e]
        gate = jnp.minimum(gu[:, :D_FF], SWIGLU_LIMIT)
        up = jnp.clip(gu[:, D_FF:], -SWIGLU_LIMIT, SWIGLU_LIMIT)
        act = (up + 1.0) * (gate * jax.nn.sigmoid(SWIGLU_ALPHA * gate))
        return act @ w_down[e] + b_down[e]

    ybuf = lax.map(expert_block, (xbuf.reshape(n_blk, EXPERT_BLOCK, d), block_e)).reshape(p_rows, d)
    out = jnp.zeros((t, d), jnp.float32).at[tbuf].add(ybuf.astype(jnp.float32) * wbuf[:, None])
    return out

def first_inputs(seed: int = 0) -> dict:
    key = jax.random.key(seed)
    ks = jax.random.split(key, 18)
    f32 = jnp.float32
    nrm = lambda k, shp: jax.random.normal(k, shp, f32)
    return {
        "x": nrm(ks[0], (BATCH, SEQ, D_MODEL)),
        "norm_mix_g": 1.0 + 0.02 * nrm(ks[1], (D_MODEL,)),
        "w_in": nrm(ks[2], (D_MODEL, IN_COLS)) * D_MODEL ** -0.5,
        "b_gate": 0.1 * nrm(ks[3], (N_BRANCHES, D_MODEL)),
        "qn_a": 1.0 + 0.02 * nrm(ks[4], (N_DIL_GROUPS, HEAD_DIM)),
        "kn_a": 1.0 + 0.02 * nrm(ks[5], (N_DIL_GROUPS, HEAD_DIM)),
        "qn_b": 1.0 + 0.02 * nrm(ks[6], (HEAD_DIM,)),
        "kn_b": 1.0 + 0.02 * nrm(ks[7], (HEAD_DIM,)),
        "w_proj_a": nrm(ks[8], (OUT_A, D_MODEL)) * OUT_A ** -0.5,
        "w_proj_b": nrm(ks[9], (OUT_B, D_MODEL)) * OUT_B ** -0.5,
        "w_out": nrm(ks[10], (D_MODEL, D_MODEL)) * D_MODEL ** -0.5,
        "norm_ffn_g": 1.0 + 0.02 * nrm(ks[11], (D_MODEL,)),
        "w_router": nrm(ks[12], (D_MODEL, N_EXPERTS)) * D_MODEL ** -0.5,
        "b_router": 0.01 * nrm(ks[13], (N_EXPERTS,)),
        "w_gate_up": nrm(ks[14], (N_EXPERTS, D_MODEL, 2 * D_FF)) * D_MODEL ** -0.5,
        "b_gate_up": 0.02 * nrm(ks[15], (N_EXPERTS, 2 * D_FF)),
        "w_down": nrm(ks[16], (N_EXPERTS, D_FF, D_MODEL)) * D_FF ** -0.5,
        "b_down": 0.02 * nrm(ks[17], (N_EXPERTS, D_MODEL)),
    }

def first_block(x, norm_mix_g, w_in, b_gate, qn_a, kn_a, qn_b, kn_b, w_proj_a, w_proj_b, w_out,
              norm_ffn_g, w_router, b_router, w_gate_up, b_gate_up, w_down, b_down):
    b, s, d = x.shape
    pos = jnp.arange(s)
    rows = s // GRID_W
    row = jnp.repeat(jnp.arange(rows), GRID_W)
    col = jnp.tile(jnp.arange(GRID_W), rows)
    split_at = list(np.cumsum([3 * WIDTH_A, WIDTH_B_Q, WIDTH_B_KV, WIDTH_B_KV]))

    for _layer in range(DEPTH):
        h = rmsnorm(x, norm_mix_g)
        proj = h @ w_in
        qkv_a, q_b, k_b, v_b, gate_logits = jnp.split(proj, split_at, axis=-1)

        qkv_a = qkv_a.reshape(b, s, 3, N_DIL_GROUPS, HEADS_A, HEAD_DIM)
        outs, lses = [], []
        for gi, (window, dil) in enumerate(DIL_PAIRS):
            qg = partial_rope(rmsnorm(qkv_a[:, :, 0, gi], qn_a[gi]), pos)
            kg = partial_rope(rmsnorm(qkv_a[:, :, 1, gi], kn_a[gi]), pos)
            og, lg = dilated_window_attention(qg, kg, qkv_a[:, :, 2, gi], window, dil)
            outs.append(og)
            lses.append(lg)
        wts = jax.nn.softmax(jnp.stack(lses, axis=0), axis=0)
        o_a = jnp.sum(wts[..., None] * jnp.stack(outs, axis=0).astype(jnp.float32), axis=0)
        o_a = o_a.astype(x.dtype).reshape(b, s, OUT_A)

        qb = axial_rope(rmsnorm(q_b.reshape(b, s, HEADS_B_Q, HEAD_DIM), qn_b), row, col)
        kb = axial_rope(rmsnorm(k_b.reshape(b, s, HEADS_B_KV, HEAD_DIM), kn_b), row, col)
        vb = v_b.reshape(b, s, HEADS_B_KV, HEAD_DIM)
        o_b = gqa_blocked_attention(qb, kb, vb)

        gates = jax.nn.sigmoid(gate_logits.reshape(b, s, N_BRANCHES, d) + b_gate)
        merged = gates[:, :, 0] * (o_a @ w_proj_a) + gates[:, :, 1] * (o_b @ w_proj_b)
        x = x + (merged @ w_out).astype(x.dtype)

        h2 = rmsnorm(x, norm_ffn_g).reshape(b * s, d)
        ff = moe_ffn(h2, w_router, b_router, w_gate_up, b_gate_up, w_down, b_down)
        x = x + ff.reshape(b, s, d).astype(x.dtype)
    return x


DEPTH_2 = 2

N_MIXERS = 3

GDN_DK = 128
GDN_DV = 128
GDN_HEADS = D_MODEL // GDN_DK
GDN_CONV = 4
GDN_CHUNK = 64
GDN_QK = GDN_HEADS * GDN_DK
GDN_V = GDN_HEADS * GDN_DV
GDN_IN = 2 * GDN_QK + 2 * GDN_V + 2 * GDN_HEADS

MOBA_DH = 128
MOBA_HEADS = D_MODEL // MOBA_DH
MOBA_BLOCK = 256
MOBA_TOPK = 3
MOBA_QBLOCK = 16
ROPE_THETA = 500000.0
ROPE_DIMS = MOBA_DH // 4

RET_DK = 256
RET_DV = 512
RET_HEADS = D_MODEL // RET_DK
RET_CHUNK = 128
XPOS_BASE = 10000.0

D_FF_2 = ((8 * D_MODEL + 3 * 256 - 1) // (3 * 256)) * 256

DEEPNORM_ALPHA = (2 * DEPTH_2) ** 0.25
DEEPNORM_BETA = (8 * DEPTH_2) ** -0.25
LN_EPS = 1e-5
NORM_EPS = 1e-6
NEG_INF = -1e30
F32 = jnp.float32


def layer_norm(x, g, b):
    xf = x.astype(F32)
    mu = jnp.mean(xf, -1, keepdims=True)
    var = jnp.mean(jnp.square(xf - mu), -1, keepdims=True)
    return ((xf - mu) * lax.rsqrt(var + LN_EPS) * g.astype(F32) + b.astype(F32)).astype(x.dtype)

def split_heads(t, n_heads):
    bsz, seq, width = t.shape
    return t.reshape(bsz, seq, n_heads, width // n_heads).transpose(0, 2, 1, 3)

def l2_normalize(t):
    tf = t.astype(F32)
    return tf * lax.rsqrt(jnp.sum(tf * tf, -1, keepdims=True) + NORM_EPS)

def apply_rotary(x, inv_freq):
    half = inv_freq.shape[0]
    seq = x.shape[2]
    ang = jnp.arange(seq, dtype=F32)[:, None] * inv_freq[None, :]
    cos, sin = jnp.cos(ang), jnp.sin(ang)
    xf = x.astype(F32)
    x1, x2 = xf[..., :half], xf[..., half:2 * half]
    out = jnp.concatenate([x1 * cos - x2 * sin, x1 * sin + x2 * cos, xf[..., 2 * half:]], -1)
    return out.astype(x.dtype)

def causal_depthwise_conv(x, w):
    width, ch = w.shape
    return lax.conv_general_dilated(
        x, w[:, None, :], window_strides=(1,), padding=[(width - 1, 0)],
        dimension_numbers=('NWC', 'WIO', 'NWC'), feature_group_count=ch)

def chunk_gated_delta_rule(q, k, v, g, beta):
    bsz, nh, seq, dk = q.shape
    dv = v.shape[-1]
    c = GDN_CHUNK
    n = seq // c
    q = q.astype(F32).reshape(bsz, nh, n, c, dk)
    k = k.astype(F32).reshape(bsz, nh, n, c, dk)
    v = v.astype(F32).reshape(bsz, nh, n, c, dv)
    gc = jnp.cumsum(g.reshape(bsz, nh, n, c), -1)
    beta = beta.reshape(bsz, nh, n, c)
    tril = jnp.tril(jnp.ones((c, c), bool))
    tril_strict = jnp.tril(jnp.ones((c, c), bool), -1)
    diff = gc[..., :, None] - gc[..., None, :]
    decay = jnp.where(tril, jnp.exp(jnp.where(tril, diff, 0.0)), 0.0)
    k_beta = k * beta[..., None]
    v_beta = v * beta[..., None]
    low = jnp.where(tril_strict, jnp.einsum('bhncd,bhnsd->bhncs', k_beta, k) * decay, 0.0)
    rhs = jnp.concatenate([v_beta, k_beta * jnp.exp(gc)[..., None]], -1)
    sol = lax.linalg.triangular_solve(low, rhs, left_side=True, lower=True, unit_diagonal=True)
    u, w = sol[..., :dv], sol[..., dv:]
    attn_intra = jnp.where(tril, jnp.einsum('bhncd,bhnsd->bhncs', q, k) * decay, 0.0)
    q_dec = q * jnp.exp(gc)[..., None]
    k_dec = k * jnp.exp(gc[..., -1:] - gc)[..., None]
    chunk_decay = jnp.exp(gc[..., -1])

    def step(state, inp):
        u_i, w_i, qd_i, kd_i, a_i, cd_i = inp
        v_new = u_i - w_i @ state
        o_i = qd_i @ state + a_i @ v_new
        state = state * cd_i[..., None, None] + jnp.swapaxes(kd_i, -1, -2) @ v_new
        return state, o_i

    xs = tuple(jnp.moveaxis(t, 2, 0) for t in (u, w, q_dec, k_dec, attn_intra, chunk_decay))
    state0 = jnp.zeros((bsz, nh, dk, dv), F32)
    _, o = lax.scan(step, state0, xs)
    return o.transpose(1, 2, 0, 3, 4).reshape(bsz, nh, seq, dv)

def gated_deltanet(x, w_in, w_conv, a_log, dt_bias, norm_g, w_out):
    bsz, seq, _ = x.shape
    nh = GDN_HEADS
    proj = x @ w_in
    qkv, z, b_logit, a_in = jnp.split(
        proj, [2 * GDN_QK + GDN_V, 2 * GDN_QK + 2 * GDN_V, 2 * GDN_QK + 2 * GDN_V + nh], axis=-1)
    qkv = jax.nn.silu(causal_depthwise_conv(qkv, w_conv))
    q, k, v = jnp.split(qkv, [GDN_QK, 2 * GDN_QK], axis=-1)
    q = l2_normalize(split_heads(q, nh)) * GDN_DK ** -0.5
    k = l2_normalize(split_heads(k, nh))
    v = split_heads(v, nh).astype(F32)
    beta = jax.nn.sigmoid(b_logit.astype(F32)).transpose(0, 2, 1)
    g = -(jnp.exp(a_log.astype(F32)) *
          jax.nn.softplus(a_in.astype(F32) + dt_bias.astype(F32))).transpose(0, 2, 1)
    o = chunk_gated_delta_rule(q, k, v, g, beta).transpose(0, 2, 1, 3)
    o = o * lax.rsqrt(jnp.mean(o * o, -1, keepdims=True) + NORM_EPS) * norm_g.astype(F32)
    o = o * jax.nn.silu(z.astype(F32)).reshape(bsz, seq, nh, GDN_DV)
    return o.reshape(bsz, seq, GDN_V).astype(x.dtype) @ w_out

def moba_attention(x, w_qkv, w_out):
    bsz, seq, _ = x.shape
    nh, dh, bs, qb = MOBA_HEADS, MOBA_DH, MOBA_BLOCK, MOBA_QBLOCK
    q, k, v = jnp.split(x @ w_qkv, 3, axis=-1)
    half = ROPE_DIMS // 2
    inv_freq = jnp.power(ROPE_THETA, -jnp.arange(half, dtype=F32) / half)
    q = apply_rotary(split_heads(q, nh), inv_freq)
    k = apply_rotary(split_heads(k, nh), inv_freq)
    v = split_heads(v, nh)
    nkb = -(-seq // bs)
    pad = nkb * bs - seq
    kp = jnp.pad(k, ((0, 0), (0, 0), (0, pad), (0, 0)))
    vp = jnp.pad(v, ((0, 0), (0, 0), (0, pad), (0, 0)))
    k_blocks = kp.reshape(bsz, nh, nkb, bs, dh)
    v_blocks = vp.reshape(bsz, nh, nkb, bs, dh)
    k_mean = jnp.mean(k_blocks.astype(F32), axis=3)
    topk = min(MOBA_TOPK, nkb)
    scale = dh ** -0.5
    b_idx = jnp.arange(bsz)[:, None, None, None]
    h_idx = jnp.arange(nh)[None, :, None, None]

    def one_query_block(qi):
        q0 = qi * qb
        own = q0 // bs
        q_blk = lax.dynamic_slice_in_dim(q, q0, qb, axis=2).astype(F32)
        gate = jnp.einsum('bhqd,bhnd->bhqn', q_blk, k_mean)
        gate = jnp.where(jnp.arange(nkb) < own, gate, -jnp.inf)
        _, sel = lax.top_k(gate, topk)
        sel_valid = sel < own
        k_sel = k_blocks[b_idx, h_idx, sel].astype(F32)
        v_sel = v_blocks[b_idx, h_idx, sel].astype(F32)
        s_sel = jnp.einsum('bhqd,bhqnkd->bhqnk', q_blk, k_sel) * scale
        s_sel = jnp.where(sel_valid[..., None], s_sel, NEG_INF)
        k_own = lax.dynamic_slice_in_dim(kp, own * bs, bs, axis=2).astype(F32)
        v_own = lax.dynamic_slice_in_dim(vp, own * bs, bs, axis=2).astype(F32)
        s_own = jnp.einsum('bhqd,bhkd->bhqk', q_blk, k_own) * scale
        q_pos = q0 + jnp.arange(qb)
        k_pos = own * bs + jnp.arange(bs)
        s_own = jnp.where(k_pos[None, :] <= q_pos[:, None], s_own, NEG_INF)
        s = jnp.concatenate([s_sel.reshape(bsz, nh, qb, topk * bs), s_own], -1)
        p = jax.nn.softmax(s, axis=-1)
        p_sel = p[..., :topk * bs].reshape(bsz, nh, qb, topk, bs)
        p_own = p[..., topk * bs:]
        return (jnp.einsum('bhqnk,bhqnkd->bhqd', p_sel, v_sel) +
                jnp.einsum('bhqk,bhkd->bhqd', p_own, v_own))

    o = lax.map(one_query_block, jnp.arange(seq // qb))
    o = o.transpose(1, 0, 3, 2, 4).reshape(bsz, seq, nh * dh)
    return o.astype(x.dtype) @ w_out

def chunk_retention(q, k, v, log_gamma):
    bsz, nh, seq, dk = q.shape
    dv = v.shape[-1]
    c = RET_CHUNK
    n = seq // c
    q = q.astype(F32).reshape(bsz, nh, n, c, dk)
    k = k.astype(F32).reshape(bsz, nh, n, c, dk)
    v = v.astype(F32).reshape(bsz, nh, n, c, dv)
    pos = jnp.arange(c, dtype=F32)
    tril = jnp.tril(jnp.ones((c, c), bool))
    rel = jnp.where(tril, pos[:, None] - pos[None, :], 0.0)
    dmat = jnp.where(tril, jnp.exp(log_gamma[:, None, None] * rel), 0.0)
    inner = jnp.einsum('bhncd,bhnsd->bhncs', q, k) * dmat[None, :, None]
    o_inner = jnp.einsum('bhncs,bhnsd->bhncd', inner, v)
    q_dec = q * jnp.exp(log_gamma[:, None] * (pos + 1.0))[None, :, None, :, None]
    k_dec = k * jnp.exp(log_gamma[:, None] * (c - 1.0 - pos))[None, :, None, :, None]
    chunk_decay = jnp.exp(log_gamma * c)[None, :, None, None]

    def step(state, inp):
        qd_i, kd_i, v_i = inp
        out = qd_i @ state
        state = state * chunk_decay + jnp.swapaxes(kd_i, -1, -2) @ v_i
        return state, out

    xs = tuple(jnp.moveaxis(t, 2, 0) for t in (q_dec, k_dec, v))
    state0 = jnp.zeros((bsz, nh, dk, dv), F32)
    _, o_cross = lax.scan(step, state0, xs)
    o = o_inner + o_cross.transpose(1, 2, 0, 3, 4)
    return o.reshape(bsz, nh, seq, dv)

def retention(x, w_in, gn_g, w_out):
    bsz, seq, _ = x.shape
    nh = RET_HEADS
    q, k, v, gate = jnp.split(x @ w_in, [nh * RET_DK, 2 * nh * RET_DK, 2 * nh * RET_DK + nh * RET_DV], axis=-1)
    inv_freq = jnp.power(XPOS_BASE, -jnp.linspace(0.0, 1.0, RET_DK // 2, dtype=F32))
    q = apply_rotary(split_heads(q, nh), inv_freq)
    k = apply_rotary(split_heads(k, nh), inv_freq).astype(F32) * RET_DK ** -0.5
    v = split_heads(v, nh)
    log_gamma = jnp.log1p(-jnp.exp2(-5.0 - jnp.arange(nh, dtype=F32)))
    o = chunk_retention(q, k, v, log_gamma).transpose(0, 2, 1, 3)
    mu = jnp.mean(o, -1, keepdims=True)
    var = jnp.mean(jnp.square(o - mu), -1, keepdims=True)
    o = ((o - mu) * lax.rsqrt(var + LN_EPS)).reshape(bsz, seq, nh * RET_DV) * gn_g.astype(F32)
    o = jax.nn.silu(gate.astype(F32)) * o
    return o.astype(x.dtype) @ w_out

def swiglu(x, w13, w2):
    g, u = jnp.split(x @ w13, 2, axis=-1)
    return (jax.nn.silu(g) * u) @ w2

def second_inputs(seed: int = 0) -> dict:
    key = jax.random.key(seed)
    ks = jax.random.split(key, 24)
    n_a = len(range(0, DEPTH_2, N_MIXERS))
    n_b = len(range(1, DEPTH_2, N_MIXERS))
    n_c = len(range(2, DEPTH_2, N_MIXERS))

    def dense(k, shape, fan_in, gain=1.0):
        return jax.random.normal(k, shape, F32) * (gain * fan_in ** -0.5)

    def gain(k, shape):
        return 1.0 + 0.02 * jax.random.normal(k, shape, F32)

    x = jax.random.normal(ks[0], (BATCH, SEQ, D_MODEL), F32)
    a_w_in = dense(ks[1], (n_a, D_MODEL, GDN_IN), D_MODEL)
    a_conv = dense(ks[2], (n_a, GDN_CONV, 2 * GDN_QK + GDN_V), GDN_CONV)
    a_a_log = jnp.log(jax.random.uniform(ks[3], (n_a, GDN_HEADS), F32, 1.0, 16.0))
    dt = jnp.exp(jax.random.uniform(ks[4], (n_a, GDN_HEADS), F32, math.log(1e-3), math.log(1e-1)))
    a_dt_bias = dt + jnp.log(-jnp.expm1(-dt))
    a_norm_g = gain(ks[5], (n_a, GDN_DV))
    a_w_out = dense(ks[6], (n_a, GDN_V, D_MODEL), GDN_V, DEEPNORM_BETA)
    b_w_qkv = dense(ks[7], (n_b, D_MODEL, 3 * MOBA_HEADS * MOBA_DH), D_MODEL)
    b_w_out = dense(ks[8], (n_b, MOBA_HEADS * MOBA_DH, D_MODEL), MOBA_HEADS * MOBA_DH, DEEPNORM_BETA)
    c_w_in = dense(ks[9], (n_c, D_MODEL, 2 * RET_HEADS * RET_DK + 2 * RET_HEADS * RET_DV), D_MODEL)
    c_gn_g = gain(ks[10], (n_c, RET_HEADS * RET_DV))
    c_w_out = dense(ks[11], (n_c, RET_HEADS * RET_DV, D_MODEL), RET_HEADS * RET_DV, DEEPNORM_BETA)
    f_w13 = dense(ks[12], (DEPTH_2, D_MODEL, 2 * D_FF_2), D_MODEL)
    f_w2 = dense(ks[13], (DEPTH_2, D_FF_2, D_MODEL), D_FF_2, DEEPNORM_BETA)
    ln1_g = gain(ks[14], (DEPTH_2, D_MODEL))
    ln1_b = 0.02 * jax.random.normal(ks[15], (DEPTH_2, D_MODEL), F32)
    ln2_g = gain(ks[16], (DEPTH_2, D_MODEL))
    ln2_b = 0.02 * jax.random.normal(ks[17], (DEPTH_2, D_MODEL), F32)
    return {'x': x, 'a_w_in': a_w_in, 'a_conv': a_conv, 'a_a_log': a_a_log, 'a_dt_bias': a_dt_bias,
            'a_norm_g': a_norm_g, 'a_w_out': a_w_out, 'b_w_qkv': b_w_qkv, 'b_w_out': b_w_out,
            'c_w_in': c_w_in, 'c_gn_g': c_gn_g, 'c_w_out': c_w_out, 'f_w13': f_w13, 'f_w2': f_w2,
            'ln1_g': ln1_g, 'ln1_b': ln1_b, 'ln2_g': ln2_g, 'ln2_b': ln2_b}

def second_block(x, a_w_in, a_conv, a_a_log, a_dt_bias, a_norm_g, a_w_out, b_w_qkv, b_w_out,
              c_w_in, c_gn_g, c_w_out, f_w13, f_w2, ln1_g, ln1_b, ln2_g, ln2_b):
    h = x
    for i in range(DEPTH_2):
        kind, j = i % N_MIXERS, i // N_MIXERS
        if kind == 0:
            mix = gated_deltanet(h, a_w_in[j], a_conv[j], a_a_log[j], a_dt_bias[j], a_norm_g[j], a_w_out[j])
        elif kind == 1:
            mix = moba_attention(h, b_w_qkv[j], b_w_out[j])
        else:
            mix = retention(h, c_w_in[j], c_gn_g[j], c_w_out[j])
        h = layer_norm(DEEPNORM_ALPHA * h + mix, ln1_g[i], ln1_b[i])
        h = layer_norm(DEEPNORM_ALPHA * h + swiglu(h, f_w13[i], f_w2[i]), ln2_g[i], ln2_b[i])
    return h


def setup_inputs(seed=0):
    out = dict(first_inputs(seed))
    for name, value in second_inputs(seed + 1).items():
        if name != "x":
            out[name + "_2"] = value
    return out


def reference(
    x, norm_mix_g, w_in, b_gate, qn_a, kn_a, qn_b, kn_b, w_proj_a, w_proj_b, w_out, norm_ffn_g,
    w_router, b_router, w_gate_up, b_gate_up, w_down, b_down, a_w_in_2, a_conv_2, a_a_log_2,
    a_dt_bias_2, a_norm_g_2, a_w_out_2, b_w_qkv_2, b_w_out_2, c_w_in_2, c_gn_g_2, c_w_out_2,
    f_w13_2, f_w2_2, ln1_g_2, ln1_b_2, ln2_g_2, ln2_b_2,
):
    x = first_block(
        x, norm_mix_g, w_in, b_gate, qn_a, kn_a, qn_b, kn_b, w_proj_a, w_proj_b, w_out,
        norm_ffn_g, w_router, b_router, w_gate_up, b_gate_up, w_down, b_down,
    )
    return second_block(
        x, a_w_in_2, a_conv_2, a_a_log_2, a_dt_bias_2, a_norm_g_2, a_w_out_2, b_w_qkv_2,
        b_w_out_2, c_w_in_2, c_gn_g_2, c_w_out_2, f_w13_2, f_w2_2, ln1_g_2, ln1_b_2, ln2_g_2,
        ln2_b_2,
    )


_drawn_inputs = setup_inputs


def setup_inputs(seed=0):
    import zlib

    import numpy as np

    out = dict(_drawn_inputs(seed))
    spreads = {}
    factors = {'qn_a': 3.053,
     'kn_a': 5.092,
     'qn_b': 3.459,
     'b_gate_up': 4.705,
     'b_down': 5.343,
     'a_norm_g_2': 22.807}
    for name, (base, spread) in spreads.items():
        noise = np.random.default_rng([zlib.crc32(name.encode()), seed]).standard_normal(out[name].shape)
        drawn = base * np.exp(spread * noise) if base else spread * noise
        out[name] = jnp.asarray(drawn.astype(out[name].dtype))
    for name, factor in factors.items():
        out[name] = (out[name] * factor).astype(out[name].dtype)
    return out
```

```python
from contextlib import ExitStack

import numpy as np

import concourse.bass as bass
from concourse import mybir

F32 = mybir.dt.float32
F32R = mybir.dt.float32r
I32 = mybir.dt.int32
U32 = mybir.dt.uint32
ALU = mybir.AluOpType
ACT = mybir.ActivationFunctionType
AX = mybir.AxisListType.X

P = 128
S = 256
NT = S // P
D = 1024
KD = D // P
HD = 64
HA = 8
NG = 3
NE = 32
FF = 1024
TOPK = 4
BLK = 64
MAXBLK = S * TOPK // BLK + NE
EPS = 1e-6
LN_EPS = 1e-5
ALPHA = (2 * 2) ** 0.25
RING = 6
SLOT = 4096
FF2 = 2816
NEG = -1e30


def shape_constants():
    t = np.arange(P)
    ident = np.eye(P)
    tri_incl = (t[:, None] <= t[None, :]) * 1.0
    tri_strict = (t[:, None] < t[None, :]) * 1.0
    count = np.broadcast_to(np.arange(64.0), (P, 64))
    pos = np.arange(S, dtype=np.float32)

    def angles(p, half, theta):
        inv = np.float32(theta) ** (-(np.arange(half, dtype=np.float32) / np.float32(half)))
        a = p[:, None] * inv[None, :].astype(np.float32)
        return np.cos(a), np.sin(a)

    c, s = angles(pos, 8, 500000.0)
    cos_a = np.concatenate([c, c, np.ones((S, 48))], 1)
    sin_a = np.concatenate([-s, s], 1)
    cr, sr = angles((np.arange(S) // 64).astype(np.float32), 16, 10000.0)
    cc, sc = angles((np.arange(S) % 64).astype(np.float32), 16, 10000.0)
    cos_b = np.concatenate([cr, cr, cc, cc], 1)
    sin_b = np.concatenate([-sr, sr, -sc, sc], 1)
    c, s = angles(pos, 16, 500000.0)
    cos_m = np.concatenate([c, c], 1)
    sin_m = np.concatenate([-s, s], 1)
    tiled = lambda a: a.reshape(NT, P, -1).transpose(1, 0, 2).reshape(P, -1)
    base = np.concatenate([ident, tri_incl, tri_strict, count] +
                          [tiled(a) for a in (cos_a, sin_a, cos_b, sin_b, cos_m, sin_m)], 1)
    q, k = np.arange(S)[:, None], np.arange(S)[None, :]
    dist = q - k
    ok = [(dist % dil == 0) & (np.abs(dist) <= window // 2)
          for window, dil in ((128, 1), (512, 4), (2048, 16))]
    mask_a = tiled(np.concatenate([np.where(m, 0.0, NEG) for m in ok], 1))
    levels = []
    for l in range(7):
        b = 1 << l
        i, j = t[None, :], t[:, None]
        levels.append((i // (2 * b) == j // (2 * b)) & (i % (2 * b) >= b) & (j % (2 * b) < b))
    causal = np.where(t[:, None] >= t[None, :], 0.0, NEG)
    late = np.concatenate([1.0 * l for l in levels] + [np.zeros((P, P)), causal], 1)
    f = lambda a: np.ascontiguousarray(a, np.float32)
    return f(base), f(mask_a), f(late)


C_IDENT, C_TRI, C_TRIS, C_COUNT = 0, 128, 256, 384
C_COSA = 448
C_SINA = C_COSA + 2 * 64
C_COSB = C_SINA + 2 * 16
C_SINB = C_COSB + 2 * 64
C_COSM = C_SINB + 2 * 64
C_SINM = C_COSM + 2 * 32
C_END = C_SINM + 2 * 32


class Signal:

    def __init__(self, sem):
        self.sem, self.count = sem, 0

    def on(self, instruction):
        instruction.then_inc(self.sem, 1)
        self.count += 1
        return self.count


W_CHUNKS = ([("q_b", 0, 4608, 512), ("kv_b", 0, 5120, 256)] +
            [(kind, g, (1536 if kind == "k_a" else 0) + 512 * g, 512)
             for g in range(NG) for kind in ("k_a", "q_a")] +
            [("v_a", g, 3072 + 512 * g, 512) for g in range(NG)] +
            [("gate", j, 5376 + 512 * j, 512) for j in range(4)])
HEAD_CHUNKS = [c for c, w in enumerate(W_CHUNKS) if w[0] in ("q_b", "kv_b", "k_a", "q_a")]
PAIR_UNITS = 8
UNITS = PAIR_UNITS + 2 * HA


def first_timeline():
    events, step = [], 0
    for c in range(len(W_CHUNKS)):
        for tile in range(NT):
            events.append(("half", c, tile, 0))
            if c >= 11:
                events.append(("attend", step))
                step += 1
            events.append(("half", c, tile, 1))
            if c - (tile == 0) in HEAD_CHUNKS and (c, tile) != (0, 0):
                events.append(("turn_heads", c - (tile == 0), 1 - tile))
            if c >= 11:
                events.append(("attend", step))
                step += 1
        if 3 <= c <= 10:
            events.append(("attend", step))
            step += 1
            if c >= 9:
                events.append(("attend", step))
                step += 1
    while step < UNITS + 2:
        events.append(("attend", step))
        step += 1
    return events


TIMELINE = first_timeline()
LAST_V = 2 * 10 + 1
GB = 3
PROJ_LOAD = len(W_CHUNKS)
OUT_LOAD = PROJ_LOAD + 2
PRE_LOADS = OUT_LOAD + 2
G_PROJ = 2 * len(W_CHUNKS)
G_OUT = G_PROJ + 8
G_MOE = G_OUT + 4


HD2 = 128
H2 = D // HD2
LOAD_QKV, LOAD_Z, LOAD_GDN_OUT = 0, 6, 8
LOAD_FFN = [10, 36]
LOAD_MOBA, LOAD_MOBA_OUT = 28, 34
POST_LOADS = 54
G_BA = G_MOE
G_QKV = G_BA + 2
G_Z = G_QKV + 24
G_GDN_OUT = G_Z + 4
G_FFN = [G_GDN_OUT + 4, G_GDN_OUT + 4 + 28 + 16]
G_MOBA = G_FFN[0] + 28
G_MOBA_OUT = G_MOBA + 12
FFN_CHUNKS = [512] * 5 + [256]
W2_PARTS = [(0, 8), (8, 16), (16, 22)]
TURN_X2 = 12
TURN_GDN = 16
TURN_LN1 = [20, 32]
TURN_MOBA_IN, TURN_MOBA_OUT = 24, 28


RAW_SLOTS = (1, 0)


def freed_after(load):
    if load < LOAD_Z:
        return G_QKV + 4 * load + 4, None
    if load < LOAD_GDN_OUT:
        return G_Z + 2 * (load - LOAD_Z) + 2, None
    if load < LOAD_FFN[0]:
        return G_GDN_OUT + 3 + (load - LOAD_GDN_OUT), None
    if LOAD_MOBA <= load < LOAD_MOBA_OUT:
        return G_MOBA + 2 * (load - LOAD_MOBA) + 2, None
    if LOAD_MOBA_OUT <= load < LOAD_FFN[1]:
        return G_MOBA_OUT + 3 + (load - LOAD_MOBA_OUT), None
    layer = 0 if load < LOAD_MOBA else 1
    i = load - LOAD_FFN[layer]
    if i < 12:
        return G_FFN[layer] + 2 * i + 2, None
    n, piece = divmod(i - 12, 3)
    if piece < 2:
        return None, 4 * layer + 2 * n + piece + 1
    return G_FFN[layer] + 24 + 2 * n + 2, None


LOAD_SHAPES = [(KD, 512)] * 10
for _layer in range(2):
    LOAD_SHAPES += [(KD, n) for n in FFN_CHUNKS for _ in range(2)]
    LOAD_SHAPES += [(b - a, 512) for _ in range(2) for a, b in W2_PARTS]
    LOAD_SHAPES += [(KD, 512)] * (8 if _layer == 0 else 0)


def gdn_timeline():
    events = []
    for m in range(24 + 4 + 6):
        if m < 24:
            events.append(("conv", m))
        elif m < 28:
            events.append(("z", m - 24))
        for n in range(8):
            at = (n // 4) * 8 + ((n // 2) % 2) * 4 + 3 + 2 + n % 2
            if m == at:
                events.append(("unit_turn", n))
            if m == at + 2:
                events.append(("unit_back", n))
        for k in range(4):
            if m == 16 + (k // 2) * 4 + 3 + 2 + k % 2:
                events.append(("v_turn", k))
        if m == 2:
            events.append(("sums", 0))
    return events


GDN_TIMELINE = gdn_timeline()
MOBA_CHUNKS = [("k", 0), ("q", 0), ("v", 0), ("k", 1), ("q", 1), ("v", 1)]
MOBA_UNITS = 2 * H2


def moba_timeline():
    events, step, turned_heads = [], 0, 0
    for c, (kind, _) in enumerate(MOBA_CHUNKS):
        for tile in range(NT):
            events.append(("half", c, tile, 0))
            done = 2 * c + tile - 1
            if done >= 0 and MOBA_CHUNKS[done // 2][0] != "v":
                events.append(("turn_heads", done // 2, done % 2))
            if c >= 3 and step < 10:
                events.append(("attend", step))
                step += 1
            if tile == 0 and c:
                events.append(("split", LOAD_MOBA + c + 1, 1))
            events.append(("half", c, tile, 1))
            if tile and c < 5:
                events.append(("split", LOAD_MOBA + c + 2, 0))
            if c >= 3 and step < 10:
                events.append(("attend", step))
                step += 1
    while step < MOBA_UNITS + 2:
        if step == 14:
            events.append(("split", LOAD_MOBA_OUT + 1, 0))
        events.append(("attend", step))
        step += 1
    return events


MOBA_TIMELINE = moba_timeline()


def slot_of(chunk):
    return (PRE_LOADS + chunk) % RING


def loads_before(slot):
    return len(range(slot, PRE_LOADS, RING))


def program(nc, t, out):
    ctx = ExitStack()
    with ctx:
        def sb(name, shape, dt=F32):
            return ctx.enter_context(nc.sbuf_tensor(name, shape, dt))

        def sem(name):
            return ctx.enter_context(nc.semaphore(name))

        base = sb("base", [P, C_END])
        late = sb("late", [P, NT * NG * S])
        res = sb("res", [P, NT, D])
        rows = sb("rows", [P, 2 * D])
        gains = sb("gains", [P, 688])
        colrows = sb("colrows", [112, P])
        cols = sb("cols", [P, 112])
        small = sb("small", [P, 512])
        tab = sb("tab", [P, 64], I32)
        top_i = sb("top_i", [P, NT, 8], U32)
        with ExitStack() as first_scope:
            def sb1(name, shape):
                return first_scope.enter_context(nc.sbuf_tensor(name, shape, F32))

            ring = sb1("ring", [P, RING, SLOT])
            actT = sb1("actT", [P, KD, S])
            arena = sb1("arena", [P, 17920])
        sb("ring_raw", [P, len(RAW_SLOTS), SLOT])
        split_w = [sb(f"split_w{i}", [P, 2, SLOT], F32R) for i in range(2)]
        act_parts = sb("act_parts", [P, 2, KD, S], F32R)
        hid_parts = sb("hid_parts", [P, 2, 22, S], F32R)
        sb("arena_rest", [P, 17920 - 13312])
        ps = ctx.enter_context(nc.psum_tensor("ps", [P, 8, 512], F32))

        def area(at, *shape):
            n = int(np.prod(shape))
            ap = arena[:, at:at + n]
            if len(shape) == 2:
                return ap.rearrange("p (a b) -> p a b", b=shape[1])
            if len(shape) == 3:
                return ap.rearrange("p (a b c) -> p a b c", b=shape[1], c=shape[2])
            return ap

        ident = base[:, C_IDENT:C_IDENT + P]
        tri = base[:, C_TRI:C_TRI + P]
        tris = base[:, C_TRIS:C_TRIS + P]
        count64 = base[:, C_COUNT:C_COUNT + 64]

        def table(at, n):
            return base[:, at:at + NT * n].rearrange("p (t n) -> p t n", n=n)

        cos_a, sin_a = table(C_COSA, 64), table(C_SINA, 16)
        cos_b, sin_b = table(C_COSB, 64), table(C_SINB, 64)
        mask_a = late[:, :].rearrange("p (t n) -> p t n", t=NT)
        qn_a = gains[:, 0:192].rearrange("p (g n) -> p g n", g=NG)
        kn_a = gains[:, 192:384].rearrange("p (g n) -> p g n", g=NG)
        qn_b, kn_b = gains[:, 384:448], gains[:, 448:512]
        b_router = gains[:, 512:544]
        mix_g, ffn_g = cols[:, 0:8], cols[:, 8:16]

        qT_a, kT_a = area(0, 12, S), area(3072, 12, S)
        v_a = area(6144, NT, 1536)
        qT_b, kT_b, v_b = area(9216, 4, S), area(10240, S), area(10496, NT, P)
        probs, probsT = area(10752, 768), area(11520, 768)
        o_a, o_b = area(9216, NT, 512), area(12288, NT, 512)
        squares = area(13312, 2, 512)
        scaled = area(14336, 512)
        heads = area(14848, 2, 512)
        swapped = area(15872, 512)
        rot_c = area(16384, 12, 64)
        rot_s = area(17152, 12, 16)
        rot_cb = area(17344, 4, 64)
        rot_sb = area(17600, 4, 64)
        gates = area(13312, NT, 2 * D)
        normed = area(0, NT, D)
        merged = area(0, NT, D)
        part = area(2048, 512)
        oT = area(3072, 2, 4 * S)

        sumsq, rstd = small[:, 0:16], small[:, 16:32]
        minus_half = small[:, 32:40]
        row_ss, row_r = small[:, 40:44], small[:, 44:48]
        peak, neg_peak = small[:, 48:50], small[:, 50:52]
        psum_ = small[:, 52:54]
        inv_sum = small[:, 54:58]
        ones_col = small[:, 58:59]
        router_w = small[:, 64:64 + KD * NE]
        ones_row = small[:, 384:512]

        x_in, const_in, col_in, gain_in, mask_in, bias_in = map(
            sem, ("x_in", "const_in", "col_in", "gain_in", "mask_in", "bias_in"))
        loaded = [sem(f"loaded{i}") for i in range(RING)]
        gemm_ready = sem("gemm_ready")
        gemm_free = [sem(f"gemm_free{i}") for i in range(GB)]
        consts_set, cols_turned, cols_ready = map(sem, ("consts_set", "cols_turned", "cols_ready"))
        row_squares, row_scale, row_normed = map(sem, ("row_squares", "row_scale", "row_normed"))
        turned, turn_done = sem("turned"), sem("turn_done")
        heads_squared, heads_summed, heads_scale, heads_ready, heads_turned, heads_evac = map(
            sem, ("heads_squared", "heads_summed", "heads_scale", "heads_ready", "heads_turned",
                  "heads_evac"))
        v_ready, gates_ready = sem("v_ready"), sem("gates_ready")
        scores_ready, peak_ready, probs_ready, probs_turned, pt_act, pt_dve, pv_done, o_ready = map(
            sem, ("scores_ready", "peak_ready", "probs_ready", "probs_turned", "pt_act", "pt_dve",
                  "pv_done", "o_ready"))
        o_turned, oT_ready, merged_ready = map(sem, ("o_turned", "oT_ready", "merged_ready"))
        v_step, a_step, p_step = sem("vector_step"), sem("scalar_step"), sem("pool_step")
        out_sent = sem("out_sent")
        (r_logits, r_onehot, r_counts, r_blocks, r_starts, r_flags, r_table, r_exp, r_weights) = map(
            sem, ("router_logits", "router_onehot", "router_counts", "router_blocks",
                  "router_starts", "router_flags", "router_table", "router_exp", "router_weights"))
        used = [sem(f"moe_used{i}") for i in range(RING)]
        bias_loaded, bias2_loaded = sem("moe_bias"), sem("moe_bias2")
        (m_sel, m_gathered, m_combined, m_gt, m_xe, m_gtsb, m_gate, m_sig, m_act, m_actp, m_turned,
         m_actT, m_y, m_seed, m_x2, m_eq, m_s, m_g4, m_g, m_dup, m_upc) = map(
            sem, ("moe_selection", "moe_gathered", "moe_combined", "moe_weights_turned",
                  "moe_rows_ready", "moe_weights_ready", "moe_gate_clipped", "moe_sigmoid",
                  "moe_act_ready", "moe_act_part", "moe_act_turned", "moe_actT_ready",
                  "moe_result_ready", "moe_seeded", "x2_ready", "moe_match", "moe_rows_chosen",
                  "moe_match_weighted", "moe_weights", "moe_weights_twice", "moe_up_clipped"))

        h2n = area(0, NT, D)
        xeT = area(2048, KD, BLK)
        gate_c, up_c, sig, act_e = area(2560, 512), area(3072, 512), area(3584, 512), area(4096, 512)
        act_eT, y_e = area(4608, 4, P), area(5120, 512)
        match, matchw = area(5632, NT * TOPK, BLK), area(6144, NT * TOPK, BLK)
        sel, weights = area(6656, NT, BLK), area(6784, NT, 2, BLK)
        weightsT = area(7040, NT, P)
        slot_at, gate_w = area(7296, NT * TOPK), area(7304, NT * TOPK)
        bias_row = area(7424, 3 * D)
        logits, top_v, top_f = area(10496, NT, NE), area(10560, NT, 8), area(10576, NT, 8)
        onehot = area(10592, NT, TOPK, NE)
        chosen, rank = area(10848, NT, NE), area(10912, NT, NE)
        picked = area(10976, NT, TOPK, NE)
        blocks_e, over = area(11232, 1), area(11240, 4)
        flags = area(11248, 64)
        ex, exsum = area(11312, NT, TOPK), area(11320, NT)
        table_f = area(11328, 64)

        loaded2 = [sem(f"loaded_second{i}") for i in range(len(RAW_SLOTS))]
        split_ready, w2_used, hid_split, mb_inverted = map(
            sem, ("weights_split", "w2_part_used", "ffn_split", "moba_inverted"))
        (late_in, ba_in, ln_in, silu_done, gd_logits, gd_soft, gd_g, gd_gc, gd_cols, gd_decay,
         un_turned, un_squared, un_summed, un_scale, un_ready, un_back, un_evac, v_turned, v_scaled,
         gd_pair, gd_diff, gd_e, gd_lt, iv_ct, iv_t1, iv_t1s, iv_y, iv_x, fin_pe, fin_dve, fin_act,
         o_squared, o_summed, o_scale, o_gated, ln_mean, ln_square, ln_scale, ln_done,
         hid_turned, hid_evac, mb_copied, mb_ready, mb_turned, mb_evac, mb_scores,
         mb_peak, mb_probs, mb_pturned, mb_pt, mb_pv, mb_o) = map(sem, (
            "late_in", "ba_in", "ln_in", "silu_done", "gdn_logits", "gdn_softplus", "gdn_log_decay",
            "gdn_cumulated", "gdn_columns", "gdn_decays", "unit_turned", "unit_squared",
            "unit_summed", "unit_scale", "unit_ready", "unit_turned_back", "unit_in_place",
            "gdn_v_turned", "gdn_v_scaled", "pair_products", "pair_differences", "pair_decays",
            "pair_ready", "inverse_level", "inverse_left", "inverse_left_copied",
            "inverse_products", "inverse_updated", "gdn_products", "gdn_vector", "gdn_copied",
            "gdn_o_squared", "gdn_o_summed", "gdn_o_scale", "gdn_o_gated", "ln_mean", "ln_square",
            "ln_scale", "ln_done", "ffn_turned", "ffn_copied",
            "moba_copied", "moba_heads", "moba_turned", "moba_in_place", "moba_scores",
            "moba_peak", "moba_probs", "moba_probs_turned", "moba_probsT", "moba_weighted",
            "moba_o"))
        levels = late[:, 0:7 * P].rearrange("p (l n) -> p l n", n=P)
        causal = late[:, 7 * P:9 * P]
        ba_w = small[:, 64:64 + KD * 16].rearrange("p (k n) -> p k n", n=16)
        a_log, dt_bias, o_gain = gains[:, 544:552], gains[:, 552:560], gains[:, 560:688]
        taps = cols[:, 16:112].rearrange("p (i m) -> p i m", m=24)
        qT, kT, vT = area(0, H2, S), area(2048, H2, S), area(4096, H2, S)
        aT = area(4096, 4, 512)
        vb = area(6144, 4, 512)
        k_dec, k_beta = area(8192, 2, 512), area(9216, 2, 512)
        o_gdn = area(8192, NT, D)
        X, XT, LT = area(10240, 4, 512), area(12288, 4, 512), area(15872, 4, 512)
        act_high, act_low = act_parts[:, 0], act_parts[:, 1]
        conv = area(10240, 2, S)
        unit_sq, unit = area(10752, 512), area(11264, 2, 512)
        decay = area(14336, 2, 512)
        level_ct, left = area(2048, 2, 512), area(3072, 2, 512)
        U0, w1T = area(2048, 2, 512), area(3072, 2, 512)
        state, U1 = area(10240, 2, 512), area(11264, 2, 512)
        z_rows = rows[:, :].rearrange("p (t n) -> p t n", t=NT)
        junk_o, junk = area(14336, D), area(13312, D)
        ln_rows = [area(15872, 2, D), rows[:, :].rearrange("p (a n) -> p a n", a=2)]
        scratch = small[:, 192:384]
        ba, nab, lsp = (scratch[:, a:a + 32].rearrange("p (t n) -> p t n", t=NT) for a in (0, 32, 64))
        beta, lg = (scratch[:, a:a + 16].rearrange("p (t n) -> p t n", t=NT) for a in (96, 112))
        cum, e_cum = scratch[:, 128:144], scratch[:, 144:160]
        rest, k_scale = scratch[:, 160:168], scratch[:, 168:176]
        bg = scratch[:, 176:184]
        e_alog = scratch[:, 184:192]
        dt16 = small[:, 0:16]
        unit_ss, unit_r = small[:, 16:24], small[:, 24:32]
        o_ss, o_r = scratch[:, 0:16], scratch[:, 16:32]
        ln_sum, ln_mu, ln_var = small[:, 40:44], small[:, 44:46], small[:, 46:48]
        hid_high, hid_low = hid_parts[:, 0], hid_parts[:, 1]
        silu_g, hidden = area(13312, 2, 512), area(14336, 2, 512)
        qT_m, kT_m, v_m = area(2048, H2, S), area(4096, H2, S), area(6144, NT, D)
        o_m = area(8192, NT, D)
        heads_m, swap_m = area(10240, 2, 512), area(11264, P)
        probs_m, probsT_m = area(11392, 2, S), area(11904, S)
        peak_m, neg_m = small[:, 48:50], small[:, 50:52]
        sum_m, inv_m = small[:, 52:54], small[:, 54:56]
        cos_m, sin_m = table(C_COSM, 32), table(C_SINM, 32)
        a_in3 = t["a_w_in_2"][0].rearrange("(k p) n -> p k n", p=P)

        w_in3 = t["w_in"].rearrange("(k p) n -> p k n", p=P)
        projs = [t[n].rearrange("(k p) n -> p k n", p=P) for n in ("w_proj_b", "w_proj_a")]
        w_out3 = t["w_out"].rearrange("(k p) n -> p k n", p=P)
        w_gu = t["w_gate_up"].rearrange("e (k p) n -> e p k n", p=P)
        w_dn = t["w_down"].rearrange("e (k p) n -> e p k n", p=P)

        def slot(i, k, n):
            return ring[:, i, 0:k * n].rearrange("p (k n) -> p k n", n=n)

        def raw_place(load, k, n):
            return slot(RAW_SLOTS[load % len(RAW_SLOTS)], k, n)

        def part_place(load, part_, k, n):
            return split_w[load % 2][:, part_, 0:k * n].rearrange("p (k n) -> p k n", n=n)

        def used_up(engine, load):
            products, parts = freed_after(load)
            if parts is None:
                engine.wait_ge(gemm_ready, products)
            else:
                engine.wait_ge(w2_used, parts)

        def expert_chunk_in(place):
            return [c for c in range(RING) if slot_of(c) == place][0]

        def everyone(name, at, n):
            return bass.AP(t[name].tensor, at, [[0, P], [1, n]])

        def read_out(engine, g):
            engine.wait_ge(gemm_free[g % GB], g // GB + 1)

        block = ctx.enter_context(nc.Block())

        @block.sync
        def _(sync):
            for tile in range(NT):
                sync.dma_start(res[:, tile], t["x"][0, tile * P:(tile + 1) * P]).then_inc(x_in, 16)
            sync.dma_start(base[:, :], t["base"]).then_inc(const_in, 16)

            def load(i, dst, src):
                sync.dma_start(dst, src).then_inc(loaded[i % RING], 16)

            for c, (_, _, at, n) in enumerate(W_CHUNKS):
                if c >= RING:
                    sync.wait_ge(gemm_ready, 2 * (c - RING) + 2)
                if c == 2:
                    sync.wait_ge(gain_in, 128)
                load(c, slot(c % RING, KD, n), w_in3[:, :, at:at + n])
            for b in range(2):
                sync.wait_ge(gemm_ready, 2 * (PROJ_LOAD + b - RING) + 2)
                load(PROJ_LOAD + b, slot((PROJ_LOAD + b) % RING, 4, D), projs[b])
            for n in range(2):
                sync.wait_ge(gemm_ready, 2 * (OUT_LOAD + n - RING) + 2)
                load(OUT_LOAD + n, slot((OUT_LOAD + n) % RING, KD, 512),
                     w_out3[:, :, n * 512:(n + 1) * 512])
            def expert_chunk(e, c):
                src = (w_gu[e, :, 4 * (c % 2):4 * (c % 2) + 4, (c // 2) * FF:(c // 2 + 1) * FF]
                       if c < 4 else w_dn[e, :, 4 * (c % 2):4 * (c % 2) + 4, :])
                s = slot_of(c)
                sync.dma_start(slot(s, 4, D), src).then_inc(loaded[s], 16)

            for c in range(RING):
                last = PRE_LOADS + c - RING
                sync.wait_ge(gemm_ready, 2 * last + 2 if last < PROJ_LOAD else
                             G_OUT if last < OUT_LOAD else G_OUT + 3 + (last - OUT_LOAD))
                expert_chunk(0, c)
            sync.wait_ge(r_table, 1)
            blocks = sync.value_load(tab[0:1, 48:49], min_val=TOPK, max_val=MAXBLK)
            with sync.Fori(1, blocks) as b:
                e = sync.value_load(tab[0:1, bass.ds(b, 1)], min_val=0, max_val=NE - 1)
                for c in range(RING):
                    sync.wait_ge(used[c], b)
                    expert_chunk(e, c)
            gdn_out, moba_in, moba_out = (t[n][0].rearrange("(k p) n -> p k n", p=P) for n in
                                          ("a_w_out_2", "b_w_qkv_2", "b_w_out_2"))
            post = [a_in3[:, :, 512 * i:512 * i + 512] for i in range(8)]
            post += [gdn_out[:, :, 512 * i:512 * i + 512] for i in range(2)]
            for layer in range(2):
                w13 = t["f_w13_2"][layer].rearrange("(k p) n -> p k n", p=P)
                w2 = t["f_w2_2"][layer].rearrange("(k p) n -> p k n", p=P)
                for j, n in enumerate(FFN_CHUNKS):
                    post += [w13[:, :, at + 512 * j:at + 512 * j + n] for at in (0, FF2)]
                post += [w2[:, a:b, 512 * n:512 * n + 512] for n in range(2)
                         for a, b in W2_PARTS]
                if layer == 0:
                    post += [moba_in[:, :, (0 if kind == "q" else D if kind == "k" else 2 * D) +
                                     512 * half:][:, :, 0:512] for kind, half in MOBA_CHUNKS]
                    post += [moba_out[:, :, 512 * i:512 * i + 512] for i in range(2)]
            assert len(post) == POST_LOADS
            for i, src in enumerate(post):
                if i < len(RAW_SLOTS):
                    sync.wait_ge(used[expert_chunk_in(RAW_SLOTS[i])], blocks)
                elif i - len(RAW_SLOTS) < LOAD_GDN_OUT:
                    used_up(sync, i - len(RAW_SLOTS))
                else:
                    sync.wait_ge(split_ready, 2 * (i - len(RAW_SLOTS) - LOAD_GDN_OUT) + 2)
                k, n = src.shape[1], src.shape[2]
                sync.dma_start(raw_place(i, k, n), src).then_inc(loaded2[i % len(RAW_SLOTS)], 16)
            for tile in range(NT):
                sync.wait_ge(ln_done, 7 + tile)
                sync.dma_start(out[0, tile * P:(tile + 1) * P], res[:, tile]).then_inc(out_sent, 16)
            sync.wait_ge(out_sent, 32)

        @block.gpsimd
        def _(pool):
            step = Signal(p_step)
            pool.memset(minus_half, -0.5).then_inc(consts_set, 1)
            pool.memset(ones_col, 1.0).then_inc(consts_set, 1)
            pool.memset(ones_row, 1.0).then_inc(consts_set, 1)
            pool.wait_ge(consts_set, 3)

            def row_scales(r):
                pool.wait_ge(row_squares, r + 1)
                c = row_r[:, r % 4:r % 4 + 1]
                n = step.on(pool.tensor_scalar(c, row_ss[:, r % 4:r % 4 + 1], 1.0 / D, EPS,
                                               ALU.mult, ALU.add))
                pool.wait_ge(p_step, n)
                pool.tensor_tensor(c, c, minus_half[:, 0:1], ALU.pow).then_inc(row_scale, 1)

            def head_scales(m, n):
                pool.wait_ge(heads_summed, m + 1)
                at = 8 * (m % 2)
                c = step.on(pool.tensor_scalar(rstd[:, at:at + n], sumsq[:, at:at + n], HD * EPS,
                                               None, ALU.add))
                pool.wait_ge(p_step, c)
                pool.tensor_tensor(rstd[:, at:at + n], rstd[:, at:at + n], minus_half[:, 0:n],
                                   ALU.pow).then_inc(heads_scale, 1)

            row_scales(0)
            row_scales(1)
            m = 0
            for c in HEAD_CHUNKS:
                for _ in range(NT):
                    head_scales(m, 2 if W_CHUNKS[c][0] == "kv_b" else 8)
                    m += 1
            row_scales(2)
            row_scales(3)
            pool.wait_ge(r_table, 1)
            blocks = pool.value_load(tab[0:1, 48:49], min_val=TOPK, max_val=MAXBLK)
            pool.dma_start(bias_row[0:1, 0:2 * FF], t["b_gate_up"][0:1, :])\
                .then_inc(bias_loaded, 16)
            pool.dma_start(bias_row[0:1, 2 * FF:3 * FF], t["b_down"][0:1, :])\
                .then_inc(bias2_loaded, 16)
            with pool.Fori(1, blocks) as b:
                e = pool.value_load(tab[0:1, bass.ds(b, 1)], min_val=0, max_val=NE - 1)
                pool.wait_ge(used[3], b)
                pool.dma_start(bias_row[0:1, 0:2 * FF],
                               t["b_gate_up"][bass.ds(e, 1), :]).then_inc(bias_loaded, 16)
                pool.wait_ge(used[5], b)
                pool.dma_start(bias_row[0:1, 2 * FF:3 * FF],
                               t["b_down"][bass.ds(e, 1), :]).then_inc(bias2_loaded, 16)

            def power(c, n, mult, add, done):
                i = step.on(pool.tensor_scalar(c, c, mult, add, ALU.mult, ALU.add))
                pool.wait_ge(p_step, i)
                pool.tensor_tensor(c, c, minus_half[:, 0:1].broadcast_to([P, n]), ALU.pow)\
                    .then_inc(done, 1)

            for n in range(8):
                pool.wait_ge(un_summed, n + 1)
                c = unit_ss[:, 4 * (n % 2):4 * (n % 2) + 4]
                power(c, 4, 1.0, EPS, un_scale)
            pool.wait_ge(late_in, 16)
            for n in range(24):
                level, group = n // 4 + 1, n % 4
                pool.wait_ge(gd_lt, group + 1)
                if n < 2:
                    pool.wait_ge(gd_lt, 4)
                else:
                    pool.wait_ge(iv_t1, n - 1)
                pool.tensor_tensor(level_ct[:, n % 2].rearrange("p (h n) -> p h n", n=P),
                                   LT[:, group].rearrange("p (h n) -> p h n", n=P),
                                   levels[:, level, None, :].broadcast_to([P, 4, P]), ALU.mult)\
                    .then_inc(iv_ct, 1)

            def ln_scales(i):
                pool.wait_ge(ln_square, i + 1)
                power(ln_var[:, i % 2:i % 2 + 1], 1, 1.0 / D, LN_EPS, ln_scale)

            for tile in range(NT):
                pool.wait_ge(o_summed, tile + 1)
                power(o_ss[:, 8 * tile:8 * tile + 8], 8, 1.0 / HD2, EPS, o_scale)
            for i in range(8):
                ln_scales(i)

        @block.tensor
        def _(pe):
            def products(g, lhs, slot_ap, k0, k1, kn, n, load, bank=None):
                bank = g % GB
                if k0 == 0:
                    if g >= GB:
                        pe.wait_ge(gemm_free[bank], g // GB)
                    pe.wait_ge(loaded[load % RING], 16 * (load // RING + 1))
                for k in range(k0, k1):
                    mm = pe.matmul(ps[:, bank, 0:n], lhs(k), slot_ap[:, k, :], start=(k == 0),
                                   stop=(k == kn - 1))
                if k1 == kn:
                    mm.then_inc(gemm_ready, 1)

            def turn(r, tile, src):
                for b in range(2):
                    for j in range(4):
                        k = 4 * b + j
                        mm = pe.transpose(ps[:, 4 + 2 * tile + b, j * P:(j + 1) * P],
                                          src[:, tile, k * P:(k + 1) * P], ident)
                    mm.then_inc(turned, 1)

            pe.wait_ge(const_in, 16)
            pe.wait_ge(col_in, 48)
            pe.transpose(ps[:, 3, 0:112], colrows[:, :], ident[0:112, 0:112]).then_inc(cols_turned, 1)
            for tile in range(NT):
                pe.wait_ge(row_normed, tile + 1)
                turn(0, tile, normed)

            def scores(u):
                if u < PAIR_UNITS:
                    pair, tile = divmod(u, 2)
                    pe.wait_ge(heads_evac, 4)
                    if u >= 2:
                        pe.wait_ge(o_ready, u - 1)
                    for kv in range(2):
                        q = slice(64 * kv, 64 * kv + 64)
                        mm = pe.matmul(ps[:, 4 + kv, 0:S], qT_b[q, pair, tile * P:(tile + 1) * P],
                                       kT_b[q, :], start=True, stop=True)
                else:
                    h, tile = divmod(u - PAIR_UNITS, 2)
                    if u == PAIR_UNITS:
                        pe.wait_ge(heads_evac, 2 * len(HEAD_CHUNKS))
                    pe.wait_ge(o_ready, u - 1)
                    q = slice(64 * (h % 2), 64 * (h % 2) + 64)
                    for g in range(NG):
                        mm = pe.matmul(ps[:, 4 + g // 2, (g % 2) * S:(g % 2 + 1) * S],
                                       qT_a[q, 4 * g + h // 2, tile * P:(tile + 1) * P],
                                       kT_a[q, 4 * g + h // 2, :], start=True, stop=True)
                mm.then_inc(scores_ready, 1)

            def turn_probs(u):
                pe.wait_ge(probs_ready, u + 1)
                for j in range(4 if u < PAIR_UNITS else 6):
                    mm = pe.transpose(ps[:, 6 + j // 4, (j % 4) * P:(j % 4 + 1) * P],
                                      probs[:, j * P:(j + 1) * P], ident)
                mm.then_inc(probs_turned, 1)

            def weighted(u):
                pe.wait_ge(pt_act, u + 1)
                pe.wait_ge(probs_ready, min(u + 2, UNITS))
                if u < PAIR_UNITS:
                    pe.wait_ge(v_ready, 2)
                    for kv in range(2):
                        for kt in range(2):
                            j = 2 * kv + kt
                            mm = pe.matmul(ps[:, 5, S + 64 * kv:S + 64 * kv + 64],
                                           probsT[:, j * P:(j + 1) * P],
                                           v_b[:, kt, 64 * kv:64 * kv + 64],
                                           start=(kt == 0), stop=(kt == 1))
                else:
                    h = (u - PAIR_UNITS) // 2
                    pe.wait_ge(pt_dve, u - PAIR_UNITS + 1)
                    if u == PAIR_UNITS:
                        for g in range(LAST_V - 2, LAST_V + 1):
                            read_out(pe, g)
                    for j in range(6):
                        g, kt = divmod(j, 2)
                        mm = pe.matmul(ps[:, 5, S:S + 64], probsT[:, j * P:(j + 1) * P],
                                       v_a[:, kt, g * 512 + h * 64:g * 512 + h * 64 + 64],
                                       start=(j == 0), stop=(j == 5))
                mm.then_inc(pv_done, 1)

            m = 0
            for event in TIMELINE:
                if event[0] == "half":
                    _, c, tile, half = event
                    if c == 0 and half == 0:
                        pe.wait_ge(turn_done, 2 * tile + 2)
                    n = W_CHUNKS[c][3]
                    products(2 * c + tile, lambda k: actT[:, k, tile * P:(tile + 1) * P],
                             slot(c % RING, KD, n), 4 * half, 4 * half + 4, KD, n, c)
                elif event[0] == "turn_heads":
                    c = event[1]
                    pe.wait_ge(heads_ready, m + 1)
                    if m:
                        pe.wait_ge(heads_evac, m)
                    for j in range(1 if W_CHUNKS[c][0] == "kv_b" else 4):
                        mm = pe.transpose(ps[:, 3, j * P:(j + 1) * P],
                                          heads[:, m % 2, j * P:(j + 1) * P], ident)
                    mm.then_inc(heads_turned, 1)
                    m += 1
                else:
                    i = event[1]
                    if 0 <= i - 2 < UNITS:
                        weighted(i - 2)
                    if 0 <= i - 1 < UNITS:
                        turn_probs(i - 1)
                    if i < UNITS:
                        scores(i)

            pe.wait_ge(o_ready, UNITS)
            for b, o in enumerate((o_b, o_a)):
                for tile in range(NT):
                    for j in range(4):
                        mm = pe.transpose(ps[:, 4 + 2 * b + tile, j * P:(j + 1) * P],
                                          o[:, tile, j * P:(j + 1) * P], ident)
                    mm.then_inc(o_turned, 1)
            pe.wait_ge(oT_ready, 4)
            g = G_PROJ
            for tile in range(NT):
                for n in range(2):
                    for b in range(2):
                        oTb = oT[:, b, :].rearrange("p (c s) -> p c s", s=S)
                        products(g, lambda k: oTb[:, k, tile * P:(tile + 1) * P],
                                 slot((PROJ_LOAD + b) % RING, 4, D)[:, :, n * 512:(n + 1) * 512],
                                 0, 4, 4, 512, PROJ_LOAD + b)
                        g += 1
            for tile in range(NT):
                pe.wait_ge(merged_ready, 2 * tile + 2)
                turn(1, tile, merged)
            for tile in range(NT):
                pe.wait_ge(turn_done, 4 + 2 * tile + 2)
                for n in range(2):
                    products(g, lambda k: actT[:, k, tile * P:(tile + 1) * P],
                             slot((OUT_LOAD + n) % RING, KD, 512), 0, KD, KD, 512, OUT_LOAD + n)
                    g += 1
            assert g == G_MOE

            for tile in range(NT):
                pe.wait_ge(row_normed, 2 + tile + 1)
                turn(2, tile, h2n)
            pe.wait_ge(r_weights, 16)
            for tile in range(NT):
                pe.wait_ge(turn_done, 8 + 2 * tile + 2)
                for k in range(KD):
                    mm = pe.matmul(ps[:, tile, 0:NE],
                                   actT[:, k, tile * P:(tile + 1) * P], router_w[:, k * NE:(k + 1) * NE],
                                   start=(k == 0), stop=(k == KD - 1))
                mm.then_inc(r_logits, 1)
            pe.wait_ge(r_onehot, 2)
            pe.matmul(ps[:, 2, 0:NE], tris, chosen[:, 0, :], start=True, stop=True)
            pe.matmul(ps[:, 2, NE:2 * NE], ones_row, chosen[:, 0, :], start=True, stop=False)
            pe.matmul(ps[:, 2, NE:2 * NE], tris, chosen[:, 1, :], start=False, stop=True)
            pe.matmul(ps[0:NE, 3, 0:1], chosen[:, 0, :], ones_col, start=True, stop=False)
            pe.matmul(ps[0:NE, 3, 0:1], chosen[:, 1, :], ones_col, start=False, stop=True)\
                .then_inc(r_counts, 1)
            pe.wait_ge(r_blocks, 1)
            nb = blocks_e[0:NE, 0:1].broadcast_to([NE, P])
            pe.matmul(ps[:, 0, 128:128 + NE], nb, tris[0:NE, 0:NE], start=True, stop=True)
            pe.matmul(ps[:, 0, 160:161], nb, ones_col[0:NE], start=True, stop=True)
            pe.matmul(ps[0:NE, 0, 192:193], tri[0:NE, 0:NE], blocks_e[0:NE, 0:1], start=True,
                      stop=True).then_inc(r_starts, 1)
            pe.wait_ge(r_flags, 1)
            pe.matmul(ps[0:1, 1, 64:64 + 48], ones_col[0:NE], flags[0:NE, 0:48], start=True,
                      stop=True).then_inc(r_starts, 1)
            for tile in range(NT):
                for n in range(2):
                    mm = pe.matmul(ps[:, 4 + 2 * tile + n, :], ident,
                                   res[:, tile, n * 512:(n + 1) * 512], start=True, stop=False,
                                   skip_group_check=True)
            mm.then_inc(m_seed, 1)

            pe.wait_ge(r_table, 1)
            blocks = pe.value_load(tab[0:1, 48:49], min_val=TOPK, max_val=MAXBLK)
            low, high = slice(0, BLK), slice(BLK, P)

            def combine():
                for tile in range(NT):
                    for n, half in enumerate((low, high)):
                        mm = pe.matmul(ps[:, 4 + 2 * tile + n, :], weightsT[half, tile, :],
                                       y_e[half, :], start=False, stop=False, skip_group_check=True)
                mm.then_inc(m_combined, 1)

            with pe.Fori(0, blocks) as b:
                def bias(bank, at):
                    for n, half in enumerate((low, high)):
                        pe.matmul(ps[half, bank, :], ones_row[0:1, 0:BLK],
                                  bias_row[0:1, at + n * 512:at + (n + 1) * 512], start=True,
                                  stop=False, skip_group_check=True)

                def chunk(bank, c, lhs):
                    s = slot_of(c)
                    pe.wait_ge(loaded[s], 16 * b + 16 * (loads_before(s) + 1))
                    w = slot(s, 4, D)
                    for k in range(4):
                        for n, half in enumerate((low, high)):
                            mm = pe.matmul(ps[half, bank, :], lhs(4 * (c % 2) + k),
                                           w[:, k, n * 512:(n + 1) * 512], start=False,
                                           stop=(k == 3 and c % 2 == 1), skip_group_check=True)
                    mm.then_inc(used[c], 1)

                pe.wait_ge(m_s, b + 1)
                for k in range(KD):
                    for tile in range(NT):
                        mm = pe.matmul(ps[:, 0, k * BLK:(k + 1) * BLK],
                                       h2n[:, tile, k * P:(k + 1) * P], sel[:, tile, :],
                                       start=(tile == 0), stop=(tile == 1), skip_group_check=True)
                mm.then_inc(m_gathered, 1)
                pe.wait_ge(m_y, b + 1)
                combine()
                pe.wait_ge(m_dup, b + 1)
                for tile in range(NT):
                    mm = pe.transpose(ps[:, 2, tile * P:(tile + 1) * P],
                                      weights[:, tile].rearrange("p a b -> p (a b)"), ident)
                mm.then_inc(m_gt, 1)
                pe.wait_ge(bias_loaded, 16 * b + 16)
                bias(1, 0)
                pe.wait_ge(m_xe, b + 1)
                for c in (0, 1):
                    chunk(1, c, lambda k: xeT[:, k, :])
                pe.wait_ge(m_gtsb, b + 2)
                bias(2, FF)
                for c in (2, 3):
                    chunk(2, c, lambda k: xeT[:, k, :])
                pe.wait_ge(bias2_loaded, 16 * b + 16)
                bias(3, 2 * FF)
                pe.wait_ge(m_act, b + 1)
                for j in range(4):
                    mm = pe.transpose(ps[:, 0, j * P:(j + 1) * P], act_e[:, j * P:(j + 1) * P], ident)
                mm.then_inc(m_turned, 1)
                pe.wait_ge(m_actT, b + 1)
                for c in (4, 5):
                    chunk(3, c, lambda k: act_eT[:, k % 4, (k // 4) * BLK:(k // 4 + 1) * BLK])
            pe.wait_ge(m_y, blocks + 1)
            combine()

            def exact(dst, left_parts, right_parts, start, stop):
                (lh, ll), (rh, rl) = left_parts, right_parts
                pe.matmul(dst, lh, rh, start=start, stop=False)
                pe.matmul(dst, lh, rl, start=False, stop=False)
                return pe.matmul(dst, ll, rh, start=False, stop=stop)

            def split_wait(load, k, kn):
                if k in (0, kn // 2):
                    pe.wait_ge(split_ready, 2 * (load - LOAD_GDN_OUT) + 1 + (k >= kn // 2))

            def second(g, lhs, load, kn, n):
                bank = g % GB
                pe.wait_ge(gemm_free[bank], g // GB)
                for k in range(kn):
                    split_wait(load, k, kn)
                    mm = exact(ps[:, bank, 0:n], lhs(k),
                               [part_place(load, i, kn, n)[:, k, :] for i in range(2)],
                               start=(k == 0), stop=(k == kn - 1))
                mm.then_inc(gemm_ready, 1)

            def tok(tile):
                s_ = slice(tile * P, (tile + 1) * P)
                return lambda k: (act_high[:, k, s_], act_low[:, k, s_])

            for tile in range(NT):
                pe.wait_ge(m_x2, 4)
                turn(3, tile, res)
            pe.wait_ge(ba_in, 16)
            for tile in range(NT):
                g = G_BA + tile
                pe.wait_ge(turn_done, TURN_X2 + 2 * tile + 2)
                pe.wait_ge(gemm_free[g % GB], g // GB)
                for k in range(KD):
                    mm = pe.matmul(ps[:, g % GB, 0:16], actT[:, k, tile * P:(tile + 1) * P],
                                   ba_w[:, k, :], start=(k == 0), stop=(k == KD - 1))
                mm.then_inc(gemm_ready, 1)

            def four(bank, src):
                for j in range(4):
                    mm = pe.transpose(ps[:, bank, j * P:(j + 1) * P], src(j), ident)
                return mm

            for kind, n in GDN_TIMELINE:
                if kind == "conv":
                    g, load = G_QKV + n, LOAD_QKV + n // 4
                    pe.wait_ge(gemm_free[g % GB], g // GB)
                    pe.wait_ge(loaded2[load % len(RAW_SLOTS)], 16 * (load // len(RAW_SLOTS) + 1))
                    for k in range(KD):
                        at = P * (n % 4)
                        mm = pe.matmul(ps[:, g % GB, 0:S], raw_place(load, KD, 512)[:, k, at:at + P],
                                       actT[:, k, :], start=(k == 0), stop=(k == KD - 1))
                    mm.then_inc(gemm_ready, 1)
                elif kind == "z":
                    g, load, tile = G_Z + n, LOAD_Z + n // 2, n % 2
                    pe.wait_ge(gemm_free[g % GB], g // GB)
                    pe.wait_ge(loaded2[load % len(RAW_SLOTS)], 16 * (load // len(RAW_SLOTS) + 1))
                    for k in range(KD):
                        mm = pe.matmul(ps[:, g % GB, :], actT[:, k, tile * P:(tile + 1) * P],
                                       raw_place(load, KD, 512)[:, k, :], start=(k == 0),
                                       stop=(k == KD - 1))
                    mm.then_inc(gemm_ready, 1)
                elif kind == "sums":
                    pe.wait_ge(gd_g, 1)
                    for tile in range(NT):
                        pe.matmul(ps[:, 3, 8 * tile:8 * tile + 8], tri, lg[:, tile, :], start=True,
                                  stop=True)
                    pe.matmul(ps[:, 3, 16:24], ones_row, lg[:, 0, :], start=True, stop=True)\
                        .then_inc(gd_gc, 1)
                elif kind == "unit_turn":
                    which, half, tile = n // 4, (n // 2) % 2, n % 2
                    pe.wait_ge(silu_done, 8 * which + 4 * half + 4)
                    if n >= 2:
                        pe.wait_ge(un_ready, n - 1)
                    src = (qT, kT)[which]
                    four(4 + n % 2, lambda j: src[:, 4 * half + j, tile * P:(tile + 1) * P])\
                        .then_inc(un_turned, 1)
                elif kind == "unit_back":
                    pe.wait_ge(un_ready, n + 1)
                    if n >= 2:
                        pe.wait_ge(un_evac, n - 1)
                    four(6 + n % 2, lambda j: unit[:, n % 2, j * P:(j + 1) * P]).then_inc(un_back, 1)
                else:
                    half, tile = n // 2, n % 2
                    pe.wait_ge(silu_done, 16 + 4 * half + 4)
                    pe.wait_ge(un_ready, 8)
                    if n >= 2:
                        pe.wait_ge(v_scaled, n - 1)
                    four(4 + n % 2, lambda j: vT[:, 4 * half + j, tile * P:(tile + 1) * P])\
                        .then_inc(v_turned, 1)

            for z in range(4):
                read_out(pe, G_Z + z)
            pe.wait_ge(un_evac, 8)
            pe.wait_ge(v_scaled, 4)
            for group in range(4):
                tile, half = divmod(group, 2)
                b = 4 * (group % 2)
                s = slice(tile * P, (tile + 1) * P)
                if group >= 2:
                    pe.wait_ge(gd_lt, group - 1)
                for j in range(4):
                    h, c = 4 * half + j, slice(j * P, (j + 1) * P)
                    pe.matmul(ps[:, b, c], lg[:, tile, h:h + 1].broadcast_to([P, P]), tri, start=True,
                              stop=True)
                    pe.matmul(ps[:, b + 1, c], beta[:, tile, h:h + 1].broadcast_to([P, P]), ident,
                              start=True, stop=True)
                    pe.matmul(ps[:, b + 2, c], kT[:, h, s], kT[:, h, s], start=True, stop=True)
                    mm = pe.matmul(ps[:, b + 3, c], kT[:, h, s], qT[:, h, s], start=True, stop=True)
                mm.then_inc(gd_pair, 1)

            pe.wait_ge(gd_lt, 4)
            for group in range(4):
                b = 4 * (group % 2)
                pe.wait_ge(iv_x, 2 * group + 1)
                if group >= 2:
                    pe.wait_ge(iv_x, 2 * (group - 2) + 2)
                four(b + 1, lambda j: XT[:, group, j * P:(j + 1) * P]).then_inc(iv_y, 1)

            def left_product(n):
                group, b = n % 4, 4 * (n % 2)
                pe.wait_ge(iv_ct, n + 1)
                pe.wait_ge(iv_x, 8 + max(n - 3, 0))
                if n >= 2:
                    pe.wait_ge(iv_t1s, n - 1)
                for j in range(4):
                    c = slice(j * P, (j + 1) * P)
                    mm = pe.matmul(ps[:, b, c], level_ct[:, n % 2, c], X[:, group, c], start=True,
                                   stop=True)
                mm.then_inc(iv_t1, 1)

            def both_products(n):
                group, b = n % 4, 4 * (n % 2)
                pe.wait_ge(iv_t1s, n + 1)
                if n >= 2:
                    pe.wait_ge(iv_x, 8 + n - 1)
                for j in range(4):
                    c = slice(j * P, (j + 1) * P)
                    if n < 20:
                        pe.matmul(ps[:, b + 1, c], XT[:, group, c], left[:, n % 2, c], start=True,
                                  stop=True)
                    mm = pe.matmul(ps[:, b + 2, c], left[:, n % 2, c], XT[:, group, c], start=True,
                                   stop=True)
                mm.then_inc(iv_y, 1)

            for n in range(24 + 2):
                if n < 24:
                    left_product(n)
                if n >= 2:
                    both_products(n - 2)

            def batch(bank, lhs, rhs, wait):
                for s_, v_ in wait:
                    pe.wait_ge(s_, v_)
                for j in range(4):
                    c = slice(j * P, (j + 1) * P)
                    mm = pe.matmul(ps[:, bank, c], lhs(c), rhs(c), start=True, stop=True)
                mm.then_inc(fin_pe, 1)

            for half in range(2):
                batch(half, lambda c: XT[:, half, c], lambda c: vb[:, half, c],
                      [(iv_x, 8 + 24)])
            for half in range(2):
                batch(2 + half, lambda c: k_beta[:, half, c], lambda c: XT[:, 2 + half, c], [])
            for half in range(2):
                batch(4 + half, lambda c: XT[:, 2 + half, c], lambda c: vb[:, 2 + half, c], [])
            for half in range(2):
                batch(6 + half, lambda c: k_dec[:, half, c], lambda c: U0[:, half, c],
                      [(fin_act, half + 1)])
            for half in range(2):
                batch(half, lambda c: w1T[:, half, c], lambda c: state[:, half, c],
                      [(fin_act, 2 + half + 1), (fin_dve, 3 + half)])
            for half in range(2):
                batch(2 + half, lambda c: qT[:, 4 * half + c.start // P, P:S], lambda c: state[:, half, c], [])
            for half in range(2):
                batch(4 + half, lambda c: aT[:, half, c], lambda c: U0[:, half, c],
                      [(fin_dve, half + 1)])
            for half in range(2):
                batch(6 + half, lambda c: aT[:, 2 + half, c], lambda c: U1[:, half, c],
                      [(fin_dve, 4 + half + 1), (fin_dve, 3 + half)])

            for tile in range(NT):
                pe.wait_ge(o_gated, tile + 1)
                turn(4, tile, o_gdn)
                pe.wait_ge(turn_done, TURN_GDN + 2 * tile + 2)
                for n in range(2):
                    second(G_GDN_OUT + 2 * tile + n, tok(tile), LOAD_GDN_OUT + n, KD, 512)

            def feed_forward(layer):
                def turn_hidden(i):
                    j, tile = divmod(i, 2)
                    read_out(pe, G_FFN[layer] + 4 * j + 2 + tile)
                    if layer + i:
                        pe.wait_ge(hid_split, 12 * layer + i)
                    for c in range(FFN_CHUNKS[j] // P):
                        mm = pe.transpose(ps[:, 3, c * P:(c + 1) * P],
                                          hidden[:, i % 2, c * P:(c + 1) * P], ident)
                    mm.then_inc(hid_turned, 1)

                g = G_FFN[layer]
                for j, n in enumerate(FFN_CHUNKS):
                    for part_ in range(2):
                        for tile in range(NT):
                            if (j, part_) == (0, 0):
                                pe.wait_ge(ln_done, 4 * layer + tile + 1)
                                turn(5, tile, res)
                                pe.wait_ge(turn_done, TURN_LN1[layer] + 2 * tile + 2)
                            second(g, tok(tile), LOAD_FFN[layer] + 2 * j + part_, KD, n)
                            g += 1
                            if j and part_ == 0:
                                turn_hidden(2 * j - 2 + tile)
                for n in range(2):
                    for piece, (k0, k1) in enumerate(W2_PARTS):
                        load = LOAD_FFN[layer] + 12 + 3 * n + piece
                        if (n, piece) == (0, 2):
                            turn_hidden(10)
                            turn_hidden(11)
                        if n == 0:
                            pe.wait_ge(hid_split, 12 * layer + 4 * (piece + 1))
                        for tile in range(NT):
                            bank = (g + tile) % GB
                            if piece == 0:
                                pe.wait_ge(gemm_free[bank], (g + tile) // GB)
                            s_ = slice(tile * P, (tile + 1) * P)
                            kn = k1 - k0
                            for k in range(kn):
                                split_wait(load, k, kn)
                                mm = exact(ps[:, bank, :],
                                           (hid_high[:, k0 + k, s_], hid_low[:, k0 + k, s_]),
                                           [part_place(load, i, kn, 512)[:, k, :] for i in range(2)],
                                           start=(k0 + k == 0), stop=(k0 + k == 21))
                            if piece == 2:
                                mm.then_inc(gemm_ready, 1)
                        if piece < 2:
                            mm.then_inc(w2_used, 1)
                    g += 2

            feed_forward(0)

            m = 0
            for event in MOBA_TIMELINE:
                if event[0] == "half":
                    _, c, tile, half = event
                    g = G_MOBA + 2 * c + tile
                    load = LOAD_MOBA + c
                    if half == 0:
                        if c == 0:
                            pe.wait_ge(ln_done, 2 + tile + 1)
                            turn(6, tile, res)
                            pe.wait_ge(turn_done, TURN_MOBA_IN + 2 * tile + 2)
                        pe.wait_ge(gemm_free[g % GB], g // GB)
                    for k in range(4 * half, 4 * half + 4):
                        split_wait(load, k, KD)
                        mm = exact(ps[:, g % GB, :], tok(tile)(k),
                                   [part_place(load, i, KD, 512)[:, k, :] for i in range(2)],
                                   start=(k == 0), stop=(k == KD - 1))
                    if half:
                        mm.then_inc(gemm_ready, 1)
                elif event[0] == "turn_heads":
                    pe.wait_ge(mb_ready, m + 1)
                    pe.wait_ge(hid_split, 12)
                    if m:
                        pe.wait_ge(mb_evac, m)
                    four(3, lambda j: heads_m[:, m % 2, j * P:(j + 1) * P]).then_inc(mb_turned, 1)
                    m += 1
                elif event[0] == "attend":
                    i = event[1]
                    if i < MOBA_UNITS:
                        h, tile = divmod(i, 2)
                        pe.wait_ge(mb_evac, 4 if h < 4 else 8)
                        if i >= 2:
                            pe.wait_ge(mb_peak, i - 1)
                        pe.matmul(ps[:, 4 + i % 2, 0:(tile + 1) * P],
                                  qT_m[:, h, tile * P:(tile + 1) * P], kT_m[:, h, 0:(tile + 1) * P],
                                  start=True, stop=True).then_inc(mb_scores, 1)
                    if 0 <= i - 2 < MOBA_UNITS:
                        u = i - 2
                        h, tile = divmod(u, 2)
                        pe.wait_ge(mb_pt, u + 1)
                        if u:
                            pe.wait_ge(mb_o, u)
                        for g in ((4, 5) if h < 4 else (10, 11)):
                            read_out(pe, G_MOBA + g)
                        for kt in range(tile + 1):
                            mm = pe.matmul(ps[:, 7, 0:P], probsT_m[:, kt * P:(kt + 1) * P],
                                           v_m[:, kt, h * P:(h + 1) * P], start=(kt == 0),
                                           stop=(kt == tile))
                        mm.then_inc(mb_pv, 1)
                    if 0 <= i - 1 < MOBA_UNITS:
                        u = i - 1
                        pe.wait_ge(mb_probs, u + 1)
                        for kt in range(u % 2 + 1):
                            mm = pe.transpose(ps[:, 6, kt * P:(kt + 1) * P],
                                              probs_m[:, u % 2, kt * P:(kt + 1) * P], ident)
                        mm.then_inc(mb_pturned, 1)
            pe.wait_ge(mb_o, MOBA_UNITS)
            turn(7, 0, o_m)
            turn(7, 1, o_m)
            for tile in range(NT):
                pe.wait_ge(turn_done, TURN_MOBA_OUT + 2 * tile + 2)
                for n in range(2):
                    second(G_MOBA_OUT + 2 * tile + n, tok(tile), LOAD_MOBA_OUT + n, KD, 512)
            feed_forward(1)

        @block.scalar
        def _(act):
            step = Signal(a_step)
            act.dma_start(colrows[0:8, :], t["norm_mix_g"].rearrange("(k p) -> k p", p=P))\
                .then_inc(col_in, 16)
            act.dma_start(colrows[8:16, :], t["norm_ffn_g"].rearrange("(k p) -> k p", p=P))\
                .then_inc(col_in, 16)
            act.dma_start(colrows[16:112, :], t["a_conv_2"][0].rearrange("i (m p) -> (i m) p", p=P))\
                .then_inc(col_in, 16)
            at = 0
            for name, n in (("qn_a", 192), ("kn_a", 192), ("qn_b", 64), ("kn_b", 64),
                            ("b_router", 32), ("a_a_log_2", 8), ("a_dt_bias_2", 8),
                            ("a_norm_g_2", 128)):
                act.dma_start(gains[:, at:at + n], everyone(name, 0, n)).then_inc(gain_in, 16)
                at += n
            act.dma_start(router_w.rearrange("p (k e) -> p k e", e=NE),
                          t["w_router"].rearrange("(k p) e -> p k e", p=P)).then_inc(r_weights, 16)
            act.dma_start(late[:, :], t["mask_a"]).then_inc(mask_in, 16)
            act.dma_start(rows[:, :], everyone("b_gate", 0, 2 * D)).then_inc(bias_in, 16)

            def row_square(r, tile):
                act.activation(squares.rearrange("p a b -> p (a b)"), res[:, tile, :], ACT.Square,
                               accum_out=row_ss[:, r % 4:r % 4 + 1]).then_inc(row_squares, 1)

            act.wait_ge(x_in, 32)
            for tile in range(NT):
                if tile:
                    act.wait_ge(row_squares, tile)
                row_square(tile, tile)

            m = 0
            e = 0
            gates_done = 0
            for event in TIMELINE:
                if event[0] == "half" and event[3] == 1:
                    _, c, tile, _ = event
                    kind, group, _, _ = W_CHUNKS[c]
                    g = 2 * c + tile
                    bank = g % GB
                    act.wait_ge(gemm_ready, g + 1)
                    if kind == "kv_b":
                        act.activation(v_b[:, tile, :], ps[:, bank, P:2 * P], ACT.Copy)\
                            .then_inc(v_ready, 1)
                    if c in HEAD_CHUNKS:
                        n = P if kind == "kv_b" else 512
                        if m == 0:
                            act.wait_ge(row_squares, 2)
                        if m >= 2:
                            act.wait_ge(heads_summed, m - 1)
                        act.activation(squares[:, m % 2, 0:n], ps[:, bank, 0:n], ACT.Square)\
                            .then_inc(heads_squared, 1)
                        m += 1
                    elif kind == "v_a":
                        act.activation(v_a[:, tile, group * 512:(group + 1) * 512], ps[:, bank, :],
                                       ACT.Copy).then_inc(gemm_free[bank], 1)
                    else:
                        act.wait_ge(gemm_free[bank], g // GB + 1)
                        s = gates[:, tile, group * 512:(group + 1) * 512]
                        act.activation(s, s, ACT.Sigmoid).then_inc(gates_ready, 1)
                elif event[0] == "turn_heads":
                    kind, group, _, _ = W_CHUNKS[event[1]]
                    tile = event[2]
                    act.wait_ge(heads_turned, e + 1)
                    s = slice(tile * P, (tile + 1) * P)
                    if kind == "kv_b":
                        dst, src = kT_b[:, s], ps[:, 3, 0:P]
                    else:
                        src = ps[:, 3, :].rearrange("p (j n) -> p j n", n=P)
                        dst = (qT_b[:, :, s] if kind == "q_b" else
                               (qT_a if kind == "q_a" else kT_a)[:, 4 * group:4 * group + 4, s])
                    act.activation(dst, src, ACT.Copy).then_inc(heads_evac, 1)
                    e += 1
                elif event[0] == "attend":
                    i = event[1]
                    if 0 <= i - 1 < UNITS:
                        act.wait_ge(probs_turned, i)
                        act.activation(probsT[:, 0:512], ps[:, 6, :], ACT.Copy).then_inc(pt_act, 1)
                    if i < UNITS:
                        act.wait_ge(peak_ready, i + 1)
                        if i >= 1:
                            act.wait_ge(probs_turned, i)
                        if i < PAIR_UNITS:
                            for kv in range(2):
                                ins = act.activation(probs[:, kv * S:(kv + 1) * S],
                                                     ps[:, 4 + kv, 0:S], ACT.Exp,
                                                     bias=neg_peak[:, kv:kv + 1], scale=HD ** -0.5,
                                                     accum_out=psum_[:, kv:kv + 1])
                        else:
                            ins = act.activation(probs, probs, ACT.Exp, bias=neg_peak[:, 0:1],
                                                 scale=HD ** -0.5, accum_out=psum_[:, 0:1])
                        ins.then_inc(probs_ready, 1)

            for b in range(2):
                act.wait_ge(o_turned, 2 * b + 1)
                act.activation(oT[:, b, :].rearrange("p (c s) -> p c s", s=S)[:, :, 0:P],
                               ps[:, 4 + 2 * b, :].rearrange("p (c s) -> p c s", s=P), ACT.Copy)\
                    .then_inc(oT_ready, 1)

            act.dma_start(late[:, 0:9 * P], t["late"]).then_inc(late_in, 16)
            for tile in range(NT):
                for n in range(2):
                    read_out(act, G_OUT + 2 * tile + n)
                if tile == 0:
                    act.wait_ge(merged_ready, 4)
                else:
                    act.wait_ge(row_squares, 3)
                row_square(2 + tile, tile)
            for tile in range(NT):
                act.wait_ge(r_exp, tile + 1)
                act.activation(ex[:, tile, :], top_v[:, tile, 0:TOPK], ACT.Exp,
                               bias=small[:, 60 + tile:61 + tile],
                               accum_out=exsum[:, tile:tile + 1]).then_inc(r_counts, 1)

            act.wait_ge(r_table, 1)
            act.dma_start(ba_w, a_in3[:, :, 4096:4112]).then_inc(ba_in, 16)
            blocks = act.value_load(tab[0:1, 48:49], min_val=TOPK, max_val=MAXBLK)
            with act.Fori(0, blocks) as b:
                act.wait_ge(m_gt, b + 1)
                act.activation(weightsT.rearrange("p a b -> p (a b)"), ps[:, 2, 0:2 * P], ACT.Copy)\
                    .then_inc(m_gtsb, 1)
                act.wait_ge(m_gate, b + 1)
                act.activation(sig, gate_c, ACT.Sigmoid, scale=1.702).then_inc(m_sig, 1)
                act.wait_ge(used[5], b + 1)
                act.activation(y_e, ps[:, 3, :], ACT.Copy).then_inc(m_y, 1)
            act.wait_ge(m_combined, blocks + 1)
            for n in range(2):
                act.activation(res[:, 0, n * 512:(n + 1) * 512], ps[:, 4 + n, :], ACT.Copy)\
                    .then_inc(m_x2, 1)

            act.wait_ge(gd_logits, 1)
            step.on(act.activation(beta, ba[:, :, 0:8], ACT.Sigmoid))
            step.on(act.activation(e_alog, a_log, ACT.Exp))
            n = step.on(act.activation(nab[:, :, 0:8], nab[:, :, 0:8], ACT.Exp))
            act.wait_ge(a_step, n)
            act.activation(lsp[:, :, 0:8], nab[:, :, 0:8], ACT.Ln, bias=ones_col).then_inc(gd_soft, 1)
            for kind, n in GDN_TIMELINE:
                if kind == "conv":
                    read_out(act, G_QKV + n)
                    act.activation((qT, kT, vT)[n // 8][:, n % 8, :], conv[:, n % 2, :], ACT.Silu)\
                        .then_inc(silu_done, 1)
                elif kind == "z":
                    g = G_Z + n
                    act.wait_ge(gemm_ready, g + 1)
                    act.activation(z_rows[:, n % 2, (n // 2) * 512:(n // 2) * 512 + 512],
                                   ps[:, g % GB, :], ACT.Silu).then_inc(gemm_free[g % GB], 1)
                elif kind == "sums":
                    act.wait_ge(gd_cols, 1)
                    step.on(act.activation(e_cum, cum, ACT.Exp))
                    act.activation(k_scale, rest, ACT.Exp).then_inc(gd_decay, 1)
                elif kind == "unit_turn":
                    act.wait_ge(un_turned, n + 1)
                    if n:
                        act.wait_ge(un_summed, n)
                    act.activation(unit_sq, ps[:, 4 + n % 2, :], ACT.Square).then_inc(un_squared, 1)
                elif kind == "unit_back":
                    which, half, tile = n // 4, (n // 2) % 2, n % 2
                    act.wait_ge(un_back, n + 1)
                    act.activation((qT, kT)[which][:, 4 * half:4 * half + 4, tile * P:(tile + 1) * P],
                                   ps[:, 6 + n % 2, :].rearrange("p (j n) -> p j n", n=P), ACT.Copy)\
                        .then_inc(un_evac, 1)
            for group in range(4):
                act.wait_ge(gd_diff, group + 1)
                act.activation(decay[:, group % 2], decay[:, group % 2], ACT.Exp).then_inc(gd_e, 1)
            for n in range(24):
                act.wait_ge(iv_t1, n + 1)
                if n >= 2:
                    act.wait_ge(iv_y, 4 + n - 1)
                act.activation(left[:, n % 2], ps[:, 4 * (n % 2), :], ACT.Copy).then_inc(iv_t1s, 1)
            for i, dst in enumerate((U0[:, 0], U0[:, 1], w1T[:, 0], w1T[:, 1])):
                act.wait_ge(fin_pe, i + 1)
                act.wait_ge(iv_y, 4 + 24)
                act.activation(dst, ps[:, i, :], ACT.Copy).then_inc(fin_act, 1)
            for tile in range(NT):
                act.wait_ge(fin_dve, 8 if tile == 0 else 12)
                if tile:
                    act.wait_ge(o_summed, tile)
                act.activation(junk_o, o_gdn[:, tile, :], ACT.Square).then_inc(o_squared, 1)

            def ln_squares(i):
                act.wait_ge(ln_mean, i + 1)
                if i % 2:
                    act.wait_ge(ln_square, i)
                act.activation(junk, res[:, i % 2, :], ACT.Square, bias=ln_mu[:, i % 2:i % 2 + 1],
                               accum_out=ln_var[:, i % 2:i % 2 + 1]).then_inc(ln_square, 1)

            def ln_load(place, g_name, b_name, layer):
                act.dma_start(ln_rows[place][:, 0, :], everyone(g_name, layer * D, D))\
                    .then_inc(ln_in, 16)
                act.dma_start(ln_rows[place][:, 1, :], everyone(b_name, layer * D, D))\
                    .then_inc(ln_in, 16)

            def feed_forward(layer):
                for i in range(12):
                    j, tile = divmod(i, 2)
                    n = FFN_CHUNKS[j]
                    g = G_FFN[layer] + 4 * j + tile
                    act.wait_ge(gemm_ready, g + 1)
                    if i == 0:
                        act.wait_ge(ln_square, 4 * layer + 2)
                    if j:
                        read_out(act, g - 2)
                    act.activation(silu_g[:, tile, 0:n], ps[:, g % GB, 0:n], ACT.Silu)\
                        .then_inc(gemm_free[g % GB], 1)
                    if j:
                        hidden_out(layer, i - 2)
                hidden_out(layer, 10)
                hidden_out(layer, 11)

            def hidden_out(layer, i):
                j, tile = divmod(i, 2)
                k = FFN_CHUNKS[j] // P
                act.wait_ge(hid_turned, 12 * layer + i + 1)
                act.activation(hid_high[:, 4 * j:4 * j + k, tile * P:(tile + 1) * P],
                               ps[:, 3, 0:k * P].rearrange("p (j n) -> p j n", n=P), ACT.Copy)\
                    .then_inc(hid_evac, 1)

            act.wait_ge(iv_ct, 24)
            ln_load(0, "ln1_g_2", "ln1_b_2", 0)
            for i in range(2):
                ln_squares(i)
            ln_load(1, "ln2_g_2", "ln2_b_2", 0)
            feed_forward(0)
            for i in range(2, 4):
                ln_squares(i)
            ln_load(0, "ln1_g_2", "ln1_b_2", 1)
            m = e = 0
            for event in MOBA_TIMELINE:
                if event[0] == "half" and event[3]:
                    _, c, tile, _ = event
                    kind, half = MOBA_CHUNKS[c]
                    g = G_MOBA + 2 * c + tile
                    act.wait_ge(gemm_ready, g + 1)
                    if kind == "v":
                        act.activation(v_m[:, tile, half * 512:(half + 1) * 512], ps[:, g % GB, :],
                                       ACT.Copy).then_inc(gemm_free[g % GB], 1)
                    else:
                        if m >= 2:
                            act.wait_ge(mb_turned, m - 1)
                        four_heads = lambda ap: ap.rearrange("p (h n) -> p h n", n=P)[:, :, 32:P]
                        act.activation(four_heads(heads_m[:, m % 2]), four_heads(ps[:, g % GB, :]),
                                       ACT.Copy).then_inc(mb_copied, 1)
                        m += 1
                elif event[0] == "turn_heads":
                    kind, half = MOBA_CHUNKS[event[1]]
                    tile = event[2]
                    act.wait_ge(mb_turned, e + 1)
                    act.activation((qT_m if kind == "q" else kT_m)
                                   [:, 4 * half:4 * half + 4, tile * P:(tile + 1) * P],
                                   ps[:, 3, :].rearrange("p (j n) -> p j n", n=P), ACT.Copy)\
                        .then_inc(mb_evac, 1)
                    e += 1
                elif event[0] == "attend":
                    i = event[1]
                    if i < MOBA_UNITS:
                        n = (i % 2 + 1) * P
                        act.wait_ge(mb_peak, i + 1)
                        if i >= 2:
                            act.wait_ge(mb_inverted, i - 1)
                        x = probs_m[:, i % 2, 0:n]
                        act.activation(x, x, ACT.Exp, bias=neg_m[:, i % 2:i % 2 + 1],
                                       scale=HD2 ** -0.5, accum_out=sum_m[:, i % 2:i % 2 + 1])\
                            .then_inc(mb_probs, 1)
                    if 0 <= i - 1 < MOBA_UNITS:
                        u = i - 1
                        n = (u % 2 + 1) * P
                        act.wait_ge(mb_pturned, u + 1)
                        if u:
                            act.wait_ge(mb_pv, u)
                        act.activation(probsT_m[:, 0:n], ps[:, 6, 0:n], ACT.Copy).then_inc(mb_pt, 1)
            for i in range(4, 6):
                ln_squares(i)
            ln_load(1, "ln2_g_2", "ln2_b_2", 1)
            feed_forward(1)
            for i in range(6, 8):
                ln_squares(i)

        @block.vector
        def _(dve):
            step = Signal(v_step)

            def after(n):
                dve.wait_ge(v_step, n)

            def turn_out(first, tile, gain):
                for b in range(2):
                    dve.wait_ge(turned, first + 2 * tile + b + 1)
                    src = ps[:, 4 + 2 * tile + b, :].rearrange("p (k n) -> p k n", n=P)
                    dst = actT[:, 4 * b:4 * b + 4, tile * P:(tile + 1) * P]
                    if gain is None:
                        ins = dve.tensor_copy(dst, src)
                    else:
                        ins = dve.tensor_tensor(dst, src, gain[:, 4 * b:4 * b + 4, None]
                                                .broadcast_to([P, 4, P]), ALU.mult)
                    ins.then_inc(turn_done, 1)

            def split(high, low, src):
                c = step.on(dve.tensor_copy(high, src))
                after(c)
                return dve.tensor_tensor(low, src, high, ALU.subtract)

            def split_half(load, half):
                k, n = LOAD_SHAPES[load]
                raw = len(RAW_SLOTS)
                if half == 0:
                    dve.wait_ge(loaded2[load % raw], 16 * (load // raw + 1))
                    if load >= LOAD_GDN_OUT + 2:
                        used_up(dve, load - 2)
                s_ = slice(half * (k // 2), k // 2 if half == 0 else k)
                split(part_place(load, 0, k, n)[:, s_, :], part_place(load, 1, k, n)[:, s_, :],
                      raw_place(load, k, n)[:, s_, :]).then_inc(split_ready, 1)

            def split_load(load):
                split_half(load, 0)
                split_half(load, 1)

            def turn_split(first, tile):
                for b in range(2):
                    dve.wait_ge(turned, first + 2 * tile + b + 1)
                    s_ = (slice(None), slice(4 * b, 4 * b + 4), slice(tile * P, (tile + 1) * P))
                    split(act_high[s_], act_low[s_],
                          ps[:, 4 + 2 * tile + b, :].rearrange("p (k n) -> p k n", n=P))\
                        .then_inc(turn_done, 1)

            dve.wait_ge(x_in, 32)
            for tile in range(NT):
                dve.wait_ge(row_scale, tile + 1)
                dve.tensor_scalar(normed[:, tile, :], res[:, tile, :], row_r[:, tile:tile + 1], None,
                                  ALU.mult).then_inc(row_normed, 1)
            dve.wait_ge(cols_turned, 1)
            dve.tensor_copy(cols[:, :], ps[:, 3, 0:112]).then_inc(cols_ready, 1)
            dve.wait_ge(cols_ready, 1)
            for tile in range(NT):
                turn_out(0, tile, mix_g)
            dve.wait_ge(const_in, 16)
            dve.wait_ge(gain_in, 128)
            root = float(HD) ** 0.5
            for i, gain in enumerate((qn_a, kn_a)):
                for g in range(NG):
                    at = (i * NG + g) * NT
                    step.on(dve.scalar_tensor_tensor(
                        rot_c[:, at:at + NT, :], cos_a, root,
                        gain[:, g, None, :].broadcast_to([P, NT, 64]), ALU.mult, ALU.mult))
                    for h in range(2):
                        other = 8 * (1 - h)
                        step.on(dve.scalar_tensor_tensor(
                            rot_s[:, at:at + NT, 8 * h:8 * h + 8], sin_a[:, :, 8 * h:8 * h + 8], root,
                            gain[:, g, None, other:other + 8].broadcast_to([P, NT, 8]),
                            ALU.mult, ALU.mult))
            for i, gain in enumerate((qn_b, kn_b)):
                step.on(dve.scalar_tensor_tensor(
                    rot_cb[:, NT * i:NT * i + NT, :], cos_b, root,
                    gain[:, None, :].broadcast_to([P, NT, 64]), ALU.mult, ALU.mult))
                for h in range(4):
                    other = 16 * (h ^ 1)
                    tables = step.on(dve.scalar_tensor_tensor(
                        rot_sb[:, NT * i:NT * i + NT, 16 * h:16 * h + 16],
                        sin_b[:, :, 16 * h:16 * h + 16], root,
                        gain[:, None, other:other + 16].broadcast_to([P, NT, 16]),
                        ALU.mult, ALU.mult))
            after(tables)

            inverted = {}
            m = 0
            for event in TIMELINE:
                if event[0] == "half" and event[3] == 1:
                    _, c, tile, _ = event
                    kind, group, _, _ = W_CHUNKS[c]
                    g = 2 * c + tile
                    bank = g % GB
                    if c in HEAD_CHUNKS:
                        nh = 2 if kind == "kv_b" else 8
                        n = nh * HD
                        at = 8 * (m % 2)
                        dve.wait_ge(heads_squared, m + 1)
                        dve.tensor_reduce(
                            sumsq[:, at:at + nh],
                            squares[:, m % 2, 0:n].rearrange("p (h e) -> p h e", e=HD), AX,
                            ALU.add).then_inc(heads_summed, 1)
                        dve.wait_ge(heads_scale, m + 1)
                        v3 = lambda ap: ap.rearrange("p (h e) -> p h e", e=HD)
                        x3 = v3(scaled[:, 0:n])
                        dve.tensor_tensor(x3, v3(ps[:, bank, 0:n]), rstd[:, at:at + nh, None]
                                          .broadcast_to([P, nh, HD]), ALU.mult)\
                            .then_inc(gemm_free[bank], 1)
                        dve.wait_ge(gemm_free[bank], g // GB + 1)
                        if m >= 2:
                            dve.wait_ge(heads_turned, m - 1)
                        isk = kind in ("kv_b", "k_a")
                        if kind in ("q_b", "kv_b"):
                            rc, rs = rot_cb[:, NT * isk + tile], rot_sb[:, NT * isk + tile]
                            width, half = HD, 16
                        else:
                            i = (isk * NG + group) * NT + tile
                            rc, rs = rot_c[:, i], rot_s[:, i]
                            width, half = 16, 8
                        if kind == "q_b":
                            y3 = heads[:, m % 2, :].rearrange("p (j k e) -> p k j e", k=2, e=HD)
                        else:
                            y3 = v3(heads[:, m % 2, 0:n])
                        sw = swapped[:, 0:nh * width].rearrange("p (h e) -> p h e", e=width)
                        if kind == "q_b":
                            for k in range(2):
                                step.on(dve.tensor_tensor(
                                    y3[:, k], x3[:, 4 * k:4 * k + 4],
                                    rc[:, None, :].broadcast_to([P, 4, HD]), ALU.mult))
                        else:
                            step.on(dve.tensor_tensor(y3, x3, rc[:, None, :]
                                                      .broadcast_to([P, nh, HD]), ALU.mult))
                        for h in range(width // half):
                            o = half * (h ^ 1)
                            last = step.on(dve.tensor_tensor(
                                sw[:, :, half * h:half * h + half], x3[:, :, o:o + half],
                                rs[:, None, half * h:half * h + half].broadcast_to([P, nh, half]),
                                ALU.mult))
                        after(last)
                        if kind == "q_b":
                            step.on(dve.tensor_tensor(y3[:, 0], y3[:, 0], sw[:, 0:4], ALU.add))
                            ins = dve.tensor_tensor(y3[:, 1], y3[:, 1], sw[:, 4:8], ALU.add)
                        else:
                            ins = dve.tensor_tensor(y3[:, :, 0:width], y3[:, :, 0:width], sw, ALU.add)
                        ins.then_inc(heads_ready, 1)
                        dve.wait_ge(heads_ready, m + 1)
                        m += 1
                    elif kind == "gate":
                        if g == 22:
                            dve.wait_ge(bias_in, 16)
                            dve.wait_ge(heads_turned, m)
                        dve.wait_ge(gemm_ready, g + 1)
                        dve.tensor_tensor(gates[:, tile, group * 512:(group + 1) * 512],
                                          ps[:, bank, :], rows[:, group * 512:(group + 1) * 512],
                                          ALU.add).then_inc(gemm_free[bank], 1)
                elif event[0] == "attend":
                    i = event[1]
                    u = i - 2
                    if 0 <= u < UNITS:
                        dve.wait_ge(pv_done, u + 1)
                        after(inverted[u])
                        inv = inv_sum[:, 2 * (u % 2):2 * (u % 2) + 2]
                        if u < PAIR_UNITS:
                            pair, tile = divmod(u, 2)
                            dst = o_b[:, tile].rearrange("p (k j e) -> p k j e", k=2, e=HD)[:, :, pair]
                            dve.tensor_tensor(dst, ps[:, 5, S:S + 128]
                                              .rearrange("p (k e) -> p k e", e=HD),
                                              inv[:, :, None].broadcast_to([P, 2, HD]), ALU.mult)\
                                .then_inc(o_ready, 1)
                        else:
                            h, tile = divmod(u - PAIR_UNITS, 2)
                            dve.tensor_scalar(o_a[:, tile, h * HD:(h + 1) * HD], ps[:, 5, S:S + HD],
                                              inv[:, 0:1], None, ALU.mult).then_inc(o_ready, 1)
                    u = i - 1
                    if 0 <= u < UNITS:
                        if u >= PAIR_UNITS:
                            dve.wait_ge(probs_turned, u + 1)
                            dve.tensor_copy(probsT[:, 512:768], ps[:, 7, 0:S]).then_inc(pt_dve, 1)
                        dve.wait_ge(probs_ready, u + 1)
                        if u >= 2:
                            dve.wait_ge(o_ready, u - 1)
                        inverted[u] = step.on(dve.reciprocal(inv_sum[:, 2 * (u % 2):2 * (u % 2) + 2],
                                                          psum_[:, 0:2]))
                    if i < UNITS:
                        dve.wait_ge(scores_ready, i + 1)
                        if i < PAIR_UNITS:
                            n = step.on(dve.tensor_reduce(peak, ps[:, 4:6, 0:S], AX, ALU.max))
                        else:
                            tile = (i - PAIR_UNITS) % 2
                            if i == PAIR_UNITS:
                                dve.wait_ge(mask_in, 16)
                            if i >= 1:
                                dve.wait_ge(probs_turned, i)
                            n = step.on(dve.tensor_tensor_reduce(
                                probs, ps[:, 4:6, :].rearrange("p a b -> p (a b)")[:, 0:768],
                                mask_a[:, tile, :], 1.0, -3e38, ALU.add, ALU.max, peak[:, 0:1]))
                        after(n)
                        dve.tensor_scalar(neg_peak, peak, -(HD ** -0.5), None, ALU.mult)\
                            .then_inc(peak_ready, 1)

            for b in range(2):
                dve.wait_ge(o_turned, 2 * b + 2)
                dve.tensor_copy(oT[:, b, :].rearrange("p (c s) -> p c s", s=S)[:, :, P:S],
                                ps[:, 5 + 2 * b, :].rearrange("p (c s) -> p c s", s=P))\
                    .then_inc(oT_ready, 1)
            dve.wait_ge(gates_ready, 8)
            g = G_PROJ
            for tile in range(NT):
                for n in range(2):
                    dst = merged[:, tile, n * 512:(n + 1) * 512]
                    dve.wait_ge(gemm_ready, g + 1)
                    dve.tensor_tensor(dst, ps[:, g % GB, :],
                                      gates[:, tile, D + n * 512:D + (n + 1) * 512], ALU.mult)\
                        .then_inc(gemm_free[g % GB], 1)
                    dve.wait_ge(gemm_free[g % GB], g // GB + 1)
                    g += 1
                    dve.wait_ge(gemm_ready, g + 1)
                    if g > G_PROJ + 1:
                        dve.wait_ge(merged_ready, 2 * tile + n)
                    dve.tensor_tensor(part, ps[:, g % GB, :],
                                      gates[:, tile, n * 512:(n + 1) * 512], ALU.mult)\
                        .then_inc(gemm_free[g % GB], 1)
                    dve.wait_ge(gemm_free[g % GB], g // GB + 1)
                    dve.tensor_tensor(dst, dst, part, ALU.add).then_inc(merged_ready, 1)
                    g += 1
            for tile in range(NT):
                turn_out(4, tile, None)
            for tile in range(NT):
                for n in range(2):
                    dve.wait_ge(gemm_ready, g + 1)
                    dst = res[:, tile, n * 512:(n + 1) * 512]
                    dve.tensor_tensor(dst, ps[:, g % GB, :], dst, ALU.add)\
                        .then_inc(gemm_free[g % GB], 1)
                    g += 1

            dve.wait_ge(merged_ready, 4)
            for tile in range(NT):
                for n in range(2):
                    read_out(dve, G_OUT + 2 * tile + n)
                dve.wait_ge(row_scale, 2 + tile + 1)
                dve.tensor_scalar(h2n[:, tile, :], res[:, tile, :], row_r[:, 2 + tile:3 + tile], None,
                                  ALU.mult).then_inc(row_normed, 1)
            for tile in range(NT):
                turn_out(8, tile, ffn_g)
            dve.memset(y_e, 0.0).then_inc(m_y, 1)
            dve.memset(weightsT, 0.0).then_inc(m_gtsb, 1)
            for tile in range(NT):
                dve.wait_ge(r_logits, tile + 1)
                n = step.on(dve.tensor_tensor(logits[:, tile, :], ps[:, tile, 0:NE],
                                              b_router, ALU.add))
                after(n)
                n = step.on(dve.max(top_v[:, tile, :], logits[:, tile, :]))
                after(n)
                dve.tensor_scalar(small[:, 60 + tile:61 + tile], top_v[:, tile, 0:1], -1.0, None,
                                  ALU.mult).then_inc(r_exp, 1)
                n = step.on(dve.max_index(top_i[:, tile, :], top_v[:, tile, :], logits[:, tile, :]))
                after(n)
                n = step.on(dve.tensor_copy(top_f[:, tile, :], top_i[:, tile, :]))
                after(n)
                n = step.on(dve.tensor_tensor(
                    onehot[:, tile], count64[:, None, 0:NE].broadcast_to([P, TOPK, NE]),
                    top_f[:, tile, 0:TOPK, None].broadcast_to([P, TOPK, NE]), ALU.is_equal))
                after(n)
                dve.tensor_reduce(chosen[:, tile, :], onehot[:, tile].rearrange("p k e -> p e k"),
                                  AX, ALU.add).then_inc(r_onehot, 1)
            dve.wait_ge(r_counts, 3)
            n = step.on(dve.tensor_copy(over[0:NE, 0:1], ps[0:NE, 3, 0:1]))
            step.on(dve.tensor_copy(rank[:, 0, :], ps[:, 2, 0:NE]))
            ranks = step.on(dve.tensor_copy(rank[:, 1, :], ps[:, 2, NE:2 * NE]))
            after(ranks)
            n = step.on(dve.tensor_scalar(flags[0:NE, 0:4], count64[0:NE, 0:4], float(BLK),
                                          over[0:NE, 0:1], ALU.mult, ALU.is_lt))
            after(n)
            n = step.on(dve.tensor_reduce(blocks_e[0:NE, :], flags[0:NE, 0:4], AX, ALU.add))
            after(n)
            dve.tensor_scalar(blocks_e[0:1, :], blocks_e[0:1, :], 1.0, None, ALU.max)\
                .then_inc(r_blocks, 1)
            dve.wait_ge(r_starts, 1)
            n = step.on(dve.tensor_copy(over[0:NE, 1:2], ps[0:NE, 0, 192:193]))
            after(n)
            dve.tensor_scalar(flags[0:NE, 0:48], count64[0:NE, 0:48], over[0:NE, 1:2], None,
                              ALU.is_ge).then_inc(r_flags, 1)
            dve.wait_ge(r_starts, 2)
            n = step.on(dve.tensor_scalar(table_f[0:1, 0:48], ps[0:1, 1, 64:112], float(NE - 1), None,
                                          ALU.min))
            step.on(dve.tensor_copy(table_f[0:1, 48:49], ps[0:1, 0, 160:161]))
            after(n + 1)
            dve.tensor_copy(tab[0:1, 0:49], table_f[0:1, 0:49]).then_inc(r_table, 1)
            for tile in range(NT):
                n = step.on(dve.scalar_tensor_tensor(rank[:, tile, :], ps[:, 0, 128:128 + NE],
                                                     float(BLK), rank[:, tile, :], ALU.mult, ALU.add))
                after(n)
                n = step.on(dve.tensor_tensor(picked[:, tile], onehot[:, tile],
                                              rank[:, tile, None, :].broadcast_to([P, TOPK, NE]),
                                              ALU.mult))
                after(n)
                n = step.on(dve.tensor_reduce(slot_at[:, tile * TOPK:(tile + 1) * TOPK],
                                              picked[:, tile], AX, ALU.add))
            n = step.on(dve.reciprocal(exsum, exsum))
            after(n)
            dve.tensor_tensor(
                gate_w.rearrange("p (t k) -> p t k", k=TOPK), ex,
                exsum[:, :, None].broadcast_to([P, NT, TOPK]), ALU.mult).then_inc(r_table, 1)
            dve.wait_ge(r_table, 2)

            blocks = dve.value_load(tab[0:1, 48:49], min_val=TOPK, max_val=MAXBLK)

            def choose(after_slots):
                dve.tensor_tensor(match, count64[:, None, :].broadcast_to([P, NT * TOPK, BLK]),
                                  slot_at[:, :, None].broadcast_to([P, NT * TOPK, BLK]),
                                  ALU.is_equal).then_inc(m_eq, 1)
                dve.wait_ge(m_eq, after_slots)
                dve.tensor_reduce(sel, match.rearrange("p (t k) s -> p t s k", k=TOPK), AX, ALU.add)\
                    .then_inc(m_s, 1)
                dve.tensor_tensor(matchw, match, gate_w[:, :, None]
                                  .broadcast_to([P, NT * TOPK, BLK]), ALU.mult).then_inc(m_g4, 1)
                dve.wait_ge(m_g4, after_slots)
                for a in range(2):
                    ins = dve.tensor_reduce(weights[:, :, a, :],
                                            matchw.rearrange("p (t k) s -> p t s k", k=TOPK), AX,
                                            ALU.add)
                ins.then_inc(m_dup, 1)
                dve.tensor_scalar(slot_at, slot_at, float(-BLK), None, ALU.add).then_inc(m_g, 1)

            choose(1)
            with dve.Fori(0, blocks) as b:
                dve.wait_ge(m_gathered, b + 1)
                dve.tensor_tensor(xeT, ps[:, 0, :].rearrange("p (k s) -> p k s", s=BLK),
                                  ffn_g[:, :, None].broadcast_to([P, KD, BLK]), ALU.mult)\
                    .then_inc(m_xe, 1)
                dve.wait_ge(used[1], b + 1)
                dve.tensor_scalar(gate_c, ps[:, 1, :], 7.0, None, ALU.min).then_inc(m_gate, 1)
                dve.wait_ge(m_g, b + 1)
                dve.wait_ge(m_gt, b + 1)
                choose(b + 2)
                dve.wait_ge(used[3], b + 1)
                dve.tensor_scalar(up_c, ps[:, 2, :], 7.0, -7.0, ALU.min, ALU.max)\
                    .then_inc(m_upc, 1)
                dve.wait_ge(m_upc, b + 1)
                dve.wait_ge(m_gate, b + 1)
                dve.scalar_tensor_tensor(up_c, up_c, 1.0, gate_c, ALU.add, ALU.mult)\
                    .then_inc(m_actp, 1)
                dve.wait_ge(m_actp, b + 1)
                dve.wait_ge(m_sig, b + 1)
                dve.tensor_tensor(act_e, up_c, sig, ALU.mult).then_inc(m_act, 1)
                dve.wait_ge(m_turned, b + 1)
                dve.tensor_copy(act_eT.rearrange("p a b -> p (a b)"), ps[:, 0, :]).then_inc(m_actT, 1)
            dve.wait_ge(m_combined, blocks + 1)
            for n in range(2):
                dve.tensor_copy(res[:, 1, n * 512:(n + 1) * 512], ps[:, 6 + n, :]).then_inc(m_x2, 1)

            n = step.on(dve.memset(dt16[:, 0:8], 0.0))
            n = step.on(dve.tensor_copy(dt16[:, 8:16], dt_bias))
            for tile in range(NT):
                turn_out(TURN_X2, tile, None)
            after(n)
            for tile in range(NT):
                g = G_BA + tile
                dve.wait_ge(gemm_ready, g + 1)
                dve.tensor_tensor(ba[:, tile, :], ps[:, g % GB, 0:16], dt16, ALU.add)\
                    .then_inc(gemm_free[g % GB], 1)
            for tile in range(NT):
                read_out(dve, G_BA + tile)
            dve.scalar_tensor_tensor(nab[:, :, 0:8], ba[:, :, 8:16], -1.0, ba[:, :, 8:16], ALU.mult,
                                     ALU.min).then_inc(gd_logits, 1)
            dve.wait_ge(gd_soft, 1)
            n = step.on(dve.scalar_tensor_tensor(lg, ba[:, :, 8:16], 0.0, lsp[:, :, 0:8], ALU.max,
                                                 ALU.add))
            after(n)
            dve.scalar_tensor_tensor(lg, lg, -1.0, e_alog[:, None, :].broadcast_to([P, NT, 8]),
                                     ALU.mult, ALU.mult).then_inc(gd_g, 1)
            four_v = lambda ap: ap.rearrange("p (j n) -> p j n", n=P)
            for kind, n in GDN_TIMELINE:
                if kind == "conv":
                    g = G_QKV + n
                    x, y = ps[:, g % GB, 0:S], conv[:, n % 2, :]
                    dve.wait_ge(gemm_ready, g + 1)
                    if n >= 2:
                        dve.wait_ge(silu_done, n - 1)
                    c = step.on(dve.tensor_scalar(y, x, taps[:, 3, n:n + 1], None, ALU.mult))
                    for back in (1, 2, 3):
                        after(c)
                        ins = dve.scalar_tensor_tensor(y[:, back:], x[:, 0:S - back],
                                                       taps[:, 3 - back, n:n + 1], y[:, back:],
                                                       ALU.mult, ALU.add)
                        if back < 3:
                            c = step.on(ins)
                    ins.then_inc(gemm_free[g % GB], 1)
                elif kind == "sums":
                    dve.wait_ge(gd_gc, 1)
                    c = step.on(dve.tensor_copy(cum, ps[:, 3, 0:16]))
                    after(c)
                    dve.tensor_tensor(rest, ps[:, 3, 16:24], cum[:, 0:8], ALU.subtract)\
                        .then_inc(gd_cols, 1)
                    dve.wait_ge(gd_decay, 1)
                    c = step.on(dve.tensor_tensor(bg, beta[:, 1, :], e_cum[:, 8:16], ALU.mult))
                    after(c)
                elif kind == "unit_turn":
                    which, half, tile = n // 4, (n // 2) % 2, n % 2
                    r = unit_ss[:, 4 * (n % 2):4 * (n % 2) + 4]
                    dve.wait_ge(un_squared, n + 1)
                    dve.tensor_reduce(r, four_v(unit_sq), AX, ALU.add).then_inc(un_summed, 1)
                    dve.wait_ge(un_scale, n + 1)
                    if n >= 2:
                        dve.wait_ge(un_back, n - 1)
                    dve.scalar_tensor_tensor(four_v(unit[:, n % 2]), four_v(ps[:, 4 + n % 2, :]),
                                             1.0 if which else HD2 ** -0.5,
                                             r[:, :, None].broadcast_to([P, 4, P]), ALU.mult,
                                             ALU.mult).then_inc(un_ready, 1)
                    dve.wait_ge(un_ready, n + 1)
                    if which:
                        by = (k_scale if tile == 0 else bg)[:, 4 * half:4 * half + 4]
                        c = step.on(dve.tensor_tensor(
                            four_v((k_dec if tile == 0 else k_beta)[:, half]), four_v(unit[:, n % 2]),
                            by[:, :, None].broadcast_to([P, 4, P]), ALU.mult))
                elif kind == "v_turn":
                    half, tile = n // 2, n % 2
                    dve.wait_ge(v_turned, n + 1)
                    dve.tensor_tensor(four_v(vb[:, 2 * tile + half]), four_v(ps[:, 4 + n % 2, :]),
                                      beta[:, tile, 4 * half:4 * half + 4, None]
                                      .broadcast_to([P, 4, P]), ALU.mult).then_inc(v_scaled, 1)
            after(c)
            for place in range(len(RAW_SLOTS), RING):
                dve.wait_ge(used[expert_chunk_in(place)], blocks)
            for z in range(4):
                read_out(dve, G_Z + z)
            c = step.on(dve.tensor_tensor(
                rows[:, :].rearrange("p (h n) -> p h n", n=P),
                rows[:, :].rearrange("p (h n) -> p h n", n=P),
                o_gain[:, None, :].broadcast_to([P, 16, P]), ALU.mult))
            dve.wait_ge(un_back, 8)
            dve.wait_ge(v_scaled, 4)
            for group in range(4):
                tile, half = divmod(group, 2)
                b = 4 * (group % 2)
                e = decay[:, group % 2]
                dve.wait_ge(gd_pair, group + 1)
                for j in range(4):
                    at = 8 * tile + 4 * half + j
                    ins = dve.tensor_scalar(e[:, j * P:(j + 1) * P], ps[:, b, j * P:(j + 1) * P],
                                            cum[:, at:at + 1], 0.0, ALU.subtract, ALU.min)
                ins.then_inc(gd_diff, 1)
                dve.wait_ge(gd_e, group + 1)
                c = step.on(dve.tensor_tensor(aT[:, group], ps[:, b + 3, :], e, ALU.mult))
                d = step.on(dve.tensor_tensor(LT[:, group], ps[:, b + 2, :], e, ALU.mult))
                after(c)
                c = step.on(dve.tensor_tensor(four_v(aT[:, group]), four_v(aT[:, group]),
                                              tri[:, None, :].broadcast_to([P, 4, P]), ALU.mult))
                after(d)
                dve.tensor_tensor(LT[:, group], LT[:, group], ps[:, b + 1, :], ALU.mult)\
                    .then_inc(gd_lt, 1)
            dve.wait_ge(late_in, 16)
            wide = ident[:, None, :].broadcast_to([P, 4, P])

            def first_left(group):
                dve.wait_ge(gd_lt, group + 1)
                c = step.on(dve.tensor_tensor(four_v(XT[:, group]), four_v(LT[:, group]),
                                              levels[:, 0, None, :].broadcast_to([P, 4, P]), ALU.mult))
                after(c)
                dve.tensor_tensor(four_v(XT[:, group]), wide, four_v(XT[:, group]), ALU.subtract)\
                    .then_inc(iv_x, 1)

            for group in range(4):
                first_left(group)
                dve.wait_ge(iv_y, group + 1)
                dve.tensor_copy(X[:, group], ps[:, 4 * (group % 2) + 1, :]).then_inc(iv_x, 1)
            for n in range(24):
                group, b = n % 4, 4 * (n % 2)
                dve.wait_ge(iv_y, 4 + n + 1)
                if n < 20:
                    step.on(dve.tensor_tensor(X[:, group], X[:, group], ps[:, b + 1, :],
                                              ALU.subtract))
                dve.tensor_tensor(XT[:, group], XT[:, group], ps[:, b + 2, :], ALU.subtract)\
                    .then_inc(iv_x, 1)
                if n in (3, 8, 13, 18):
                    split_half(LOAD_GDN_OUT + n // 10, int(n in (8, 18)))
            dve.wait_ge(iv_y, 4 + 24)
            for half in range(2):
                dve.wait_ge(fin_pe, 5 + half)
                dve.tensor_copy(U1[:, half], ps[:, 4 + half, :]).then_inc(fin_dve, 1)
            for half in range(2):
                dve.wait_ge(fin_pe, 7 + half)
                dve.tensor_copy(state[:, half], ps[:, 6 + half, :]).then_inc(fin_dve, 1)
            dve.wait_ge(fin_dve, 2)
            for half in range(2):
                dve.wait_ge(fin_pe, 9 + half)
                dve.tensor_tensor(U1[:, half], U1[:, half], ps[:, half, :], ALU.subtract)\
                    .then_inc(fin_dve, 1)
            o_half = lambda tile, half: o_gdn[:, tile, half * 512:(half + 1) * 512]
            for half in range(2):
                dve.wait_ge(fin_pe, 13 + half)
                dve.tensor_copy(o_half(0, half), ps[:, 4 + half, :]).then_inc(fin_dve, 1)
            for half in range(2):
                dve.wait_ge(fin_pe, 11 + half)
                dve.tensor_tensor(four_v(o_half(1, half)), four_v(ps[:, 2 + half, :]),
                                  e_cum[:, 8 + 4 * half:12 + 4 * half, None].broadcast_to([P, 4, P]),
                                  ALU.mult).then_inc(fin_dve, 1)
            for half in range(2):
                dve.wait_ge(fin_dve, 9 + half)
                dve.wait_ge(fin_pe, 15 + half)
                dve.tensor_tensor(o_half(1, half), o_half(1, half), ps[:, 6 + half, :], ALU.add)\
                    .then_inc(fin_dve, 1)
            eight = lambda ap: ap.rearrange("p (h n) -> p h n", n=P)
            for tile in range(NT):
                dve.wait_ge(o_squared, tile + 1)
                dve.tensor_reduce(o_ss[:, 8 * tile:8 * tile + 8], eight(junk_o), AX, ALU.add)\
                    .then_inc(o_summed, 1)
                if tile:
                    turn_split(TURN_GDN, 0)
                dve.wait_ge(o_scale, tile + 1)
                o3 = eight(o_gdn[:, tile, :])
                c = step.on(dve.tensor_tensor(o3, o3, o_ss[:, 8 * tile:8 * tile + 8, None]
                                              .broadcast_to([P, 8, P]), ALU.mult))
                after(c)
                dve.tensor_tensor(o_gdn[:, tile, :], o_gdn[:, tile, :], z_rows[:, tile, :], ALU.mult)\
                    .then_inc(o_gated, 1)
            turn_split(TURN_GDN, 1)

            def ln_add(tile, n, g):
                dve.wait_ge(gemm_ready, g + 1)
                part_ = res[:, tile, n * 512:(n + 1) * 512]
                dve.scalar_tensor_tensor(part_, part_, ALPHA, ps[:, g % GB, :], ALU.mult, ALU.add,
                                         accum_out=ln_sum[:, 2 * tile + n:2 * tile + n + 1])\
                    .then_inc(gemm_free[g % GB], 1)

            def layer_norm(i, products, place, meanwhile=None):
                tile = i % 2
                x = res[:, tile, :]
                for g in products:
                    read_out(dve, g)
                mu = ln_mu[:, tile:tile + 1]
                c = step.on(dve.tensor_tensor(mu, ln_sum[:, 2 * tile:2 * tile + 1],
                                              ln_sum[:, 2 * tile + 1:2 * tile + 2], ALU.add))
                after(c)
                dve.tensor_scalar(mu, mu, -1.0 / D, None, ALU.mult).then_inc(ln_mean, 1)
                if meanwhile:
                    meanwhile()
                dve.wait_ge(ln_scale, i + 1)
                c = step.on(dve.tensor_scalar(x, x, mu, ln_var[:, tile:tile + 1], ALU.add, ALU.mult))
                after(c)
                dve.wait_ge(ln_in, 32 * (i // 2 + 1))
                c = step.on(dve.tensor_tensor(x, x, ln_rows[place][:, 0, :], ALU.mult))
                after(c)
                dve.tensor_tensor(x, x, ln_rows[place][:, 1, :], ALU.add).then_inc(ln_done, 1)

            def mixer_norm(layer, g):
                for tile in range(NT):
                    for n in range(2):
                        ln_add(tile, n, g + 2 * tile + n)
                        if (tile, n) == (1, 0):
                            split_load(LOAD_FFN[layer])
                    layer_norm(4 * layer + tile, (g + 2 * tile, g + 2 * tile + 1), 0,
                               (lambda: turn_split(TURN_LN1[layer], 0)) if tile else None)

            def feed_forward(layer, next_load):
                first = LOAD_FFN[layer]

                def hidden_split(i):
                    j, tile = divmod(i, 2)
                    k = FFN_CHUNKS[j] // P
                    s_ = (slice(None), slice(4 * j, 4 * j + k), slice(tile * P, (tile + 1) * P))
                    dve.wait_ge(hid_evac, 12 * layer + i + 1)
                    dve.tensor_tensor(hid_low[s_], ps[:, 3, 0:k * P]
                                      .rearrange("p (j n) -> p j n", n=P), hid_high[s_],
                                      ALU.subtract).then_inc(hid_split, 1)

                turn_split(TURN_LN1[layer], 1)
                split_load(first + 1)
                for j, n in enumerate(FFN_CHUNKS):
                    if j:
                        hidden_split(2 * j - 2)
                        hidden_split(2 * j - 1)
                    split_load(first + 2 * j + 2)
                    for tile in range(NT):
                        i = 2 * j + tile
                        g = G_FFN[layer] + 4 * j + tile
                        read_out(dve, g)
                        dve.wait_ge(gemm_ready, g + 3)
                        if i >= 2:
                            dve.wait_ge(hid_turned, 12 * layer + i - 1)
                        dve.tensor_tensor(hidden[:, tile, 0:n], silu_g[:, tile, 0:n],
                                          ps[:, (g + 2) % GB, 0:n], ALU.mult)\
                            .then_inc(gemm_free[(g + 2) % GB], 1)
                    split_load(first + 2 * j + 3)
                g = G_FFN[layer] + 24
                split_load(first + 14)
                hidden_split(10)
                hidden_split(11)
                split_load(first + 15)
                for tile in range(NT):
                    ln_add(tile, 0, g + tile)
                split_load(first + 16)
                split_load(first + 17)
                if next_load:
                    split_load(next_load)
                for tile in range(NT):
                    ln_add(tile, 1, g + 2 + tile)
                for tile in range(NT):
                    layer_norm(4 * layer + 2 + tile, (g + tile, g + 2 + tile), 1,
                               (lambda: turn_split(TURN_MOBA_IN, 0)) if tile and next_load else None)

            mixer_norm(0, G_GDN_OUT)
            feed_forward(0, LOAD_MOBA)
            turn_split(TURN_MOBA_IN, 1)
            split_load(LOAD_MOBA + 1)
            m = 0
            for event in MOBA_TIMELINE:
                if event[0] == "half" and event[3]:
                    _, c, tile, _ = event
                    kind, half = MOBA_CHUNKS[c]
                    g = G_MOBA + 2 * c + tile
                    if kind == "v":
                        continue
                    dve.wait_ge(gemm_ready, g + 1)
                    dve.wait_ge(mb_copied, m + 1)
                    if m >= 2:
                        dve.wait_ge(mb_turned, m - 1)
                    x3, y3 = four_v(ps[:, g % GB, :]), four_v(heads_m[:, m % 2])
                    sw = swap_m.rearrange("p (h n) -> p h n", n=32)
                    step.on(dve.tensor_tensor(y3[:, :, 0:32], x3[:, :, 0:32],
                                              cos_m[:, tile, None, :].broadcast_to([P, 4, 32]),
                                              ALU.mult))
                    if m:
                        dve.wait_ge(mb_ready, m)
                    step.on(dve.tensor_tensor(sw[:, :, 0:16], x3[:, :, 16:32],
                                              sin_m[:, tile, None, 0:16].broadcast_to([P, 4, 16]),
                                              ALU.mult))
                    dve.tensor_tensor(sw[:, :, 16:32], x3[:, :, 0:16],
                                      sin_m[:, tile, None, 16:32].broadcast_to([P, 4, 16]),
                                      ALU.mult).then_inc(gemm_free[g % GB], 1)
                    read_out(dve, g)
                    dve.tensor_tensor(y3[:, :, 0:32], y3[:, :, 0:32], sw, ALU.add)\
                        .then_inc(mb_ready, 1)
                    m += 1
                elif event[0] == "split":
                    split_half(event[1], event[2])
                elif event[0] == "attend":
                    i = event[1]
                    if i < MOBA_UNITS:
                        tile = i % 2
                        n = (tile + 1) * P
                        dve.wait_ge(mb_scores, i + 1)
                        if i >= 2:
                            dve.wait_ge(mb_pturned, i - 1)
                            dve.wait_ge(mb_probs, i - 1)
                        peak_i, neg_i = (v[:, i % 2:i % 2 + 1] for v in (peak_m, neg_m))
                        c = step.on(dve.tensor_tensor_reduce(
                            probs_m[:, i % 2, 0:n], ps[:, 4 + i % 2, 0:n],
                            causal[:, 2 * P - n:2 * P], 1.0, -3e38, ALU.add, ALU.max, peak_i))
                        after(c)
                        dve.tensor_scalar(neg_i, peak_i, -(HD2 ** -0.5), None, ALU.mult)\
                            .then_inc(mb_peak, 1)
                    u = i - 2
                    if 0 <= u < MOBA_UNITS:
                        h, tile = divmod(u, 2)
                        dve.wait_ge(mb_pv, u + 1)
                        dve.wait_ge(mb_inverted, u + 1)
                        dve.tensor_scalar(o_m[:, tile, h * P:(h + 1) * P], ps[:, 7, 0:P],
                                          inv_m[:, u % 2:u % 2 + 1], None, ALU.mult)\
                            .then_inc(mb_o, 1)
                    u = i - 1
                    if 0 <= u < MOBA_UNITS:
                        dve.wait_ge(mb_probs, u + 1)
                        if u >= 2:
                            dve.wait_ge(mb_o, u - 1)
                        dve.reciprocal(inv_m[:, u % 2:u % 2 + 1], sum_m[:, u % 2:u % 2 + 1])\
                            .then_inc(mb_inverted, 1)
            for tile in range(NT):
                turn_split(TURN_MOBA_OUT, tile)
            split_half(LOAD_MOBA_OUT + 1, 1)
            mixer_norm(1, G_MOBA_OUT)
            feed_forward(1, None)


_INS = ["x", "norm_mix_g", "w_in", "b_gate", "qn_a", "kn_a", "qn_b", "kn_b", "w_proj_a", "w_proj_b",
        "w_out", "norm_ffn_g", "w_router", "b_router", "w_gate_up", "b_gate_up", "w_down", "b_down",
        "a_w_in_2", "a_conv_2", "a_a_log_2", "a_dt_bias_2", "a_norm_g_2", "a_w_out_2", "b_w_qkv_2",
        "b_w_out_2", "f_w13_2", "f_w2_2", "ln1_g_2", "ln1_b_2", "ln2_g_2", "ln2_b_2"]


def kernel(**inputs):
    import numpy as _np
    import concourse.bacc as _bacc
    from concourse import mybir as _mybir
    from concourse.bass_utils import run_bass_kernel_spmd as _run

    nc = _bacc.Bacc("TRN2", target_bir_lowering=False, num_devices=1)
    arrays, t = {}, {}
    data = {name: _np.ascontiguousarray(inputs[name]) for name in _INS}
    data.update(zip(("base", "mask_a", "late"), shape_constants()))
    for name, a in data.items():
        arrays[f"in_{name}_dram"] = a
        t[name] = nc.dram_tensor(f"in_{name}_dram", a.shape, _mybir.dt.from_np(a.dtype),
                                 kind="ExternalInput").ap()
    out = nc.dram_tensor("out_0_dram", (1, S, D), _mybir.dt.float32, kind="ExternalOutput").ap()
    program(nc, t, out)
    r = _run(nc, [arrays], core_ids=[0])
    return r.results[0]["out_0_dram"]
```
